# Optimizing a Trainium2 kernel written in Bass

```python
import math
import jax, jax.numpy as jnp
from jax import lax
import numpy as np

D_MODEL = 2048
BATCH = 1
SEQ = 512
DEPTH = 1

CHUNK = 64
EPS = 1e-6

POOL_WINDOWS = (2, 4, 8, 16)
POOL_GROUPS = len(POOL_WINDOWS)
POOL_WIDTH = D_MODEL // 4
POOL_GC = POOL_WIDTH // POOL_GROUPS

CONV_WIDTH = D_MODEL // 4
CONV_K = 3

ATTN_HEADS = 8
HEAD_DIM = D_MODEL // 16
ATTN_WIDTH = ATTN_HEADS * HEAD_DIM
IDX_HEADS = 8
IDX_DIM = 64
TOPK_MAX = 256
QBLOCK = 128

N_BRANCH = 3
D_FF = 4 * D_MODEL

COL_SIZES = (
    POOL_WIDTH,
    CONV_WIDTH,
    CONV_WIDTH,
    CONV_WIDTH,
    ATTN_WIDTH,
    ATTN_WIDTH,
    ATTN_WIDTH,
    IDX_HEADS * IDX_DIM,
    IDX_DIM,
    IDX_HEADS,
    N_BRANCH * D_MODEL,
)
IN_WIDTH = sum(COL_SIZES)

kernel_name = "hybrid_pool_conv_dsa_block"

def _split_points():
    pts, acc = [], 0
    for c in COL_SIZES[:-1]:
        acc += c
        pts.append(acc)
    return pts

def _rmsnorm(x, g):
    xf = x.astype(jnp.float32)
    y = xf * lax.rsqrt(jnp.mean(xf * xf, axis=-1, keepdims=True) + EPS) * g.astype(jnp.float32)
    return y.astype(x.dtype)

def _multiscale_pool(u, pool_w, pool_scale):
    B, S, P = u.shape
    uf = u.astype(jnp.float32)
    cs = jnp.concatenate([jnp.zeros((B, 1, P), jnp.float32), jnp.cumsum(uf, axis=1)], axis=1)
    t = jnp.arange(S)
    outs = []
    for g, w in enumerate(POOL_WINDOWS):
        sl = slice(g * POOL_GC, (g + 1) * POOL_GC)
        lo = jnp.maximum(t + 1 - w, 0)
        total = cs[:, 1:, sl] - jnp.take(cs[:, :, sl], lo, axis=1)
        cnt = jnp.minimum(t + 1, w).astype(jnp.float32)[None, :, None]
        outs.append(total / cnt - uf[..., sl])
    d = jnp.stack(outs, axis=2)
    y = jnp.einsum('bsgc,gcd->bsgd', d, pool_w.astype(jnp.float32)).reshape(B, S, P)
    return (y * pool_scale.astype(jnp.float32)).astype(u.dtype)

def _short_conv(bg, cg, xin, conv_w):
    S = xin.shape[1]
    z = cg * xin
    zp = jnp.pad(z, ((0, 0), (CONV_K - 1, 0), (0, 0)))
    y = conv_w[0] * zp[:, 0:S]
    for j in range(1, CONV_K):
        y = y + conv_w[j] * zp[:, j:j + S]
    return bg * y

def _sparse_attention(q, k, v, qi, ki, wi, topk):
    B, S = q.shape[0], q.shape[1]
    nb = S // QBLOCK
    key_chunk = jnp.arange(S) // CHUNK

    def per_seq(q1, k1, v1, qi1, ki1, wi1):
        qb = q1.reshape(nb, QBLOCK, ATTN_HEADS, HEAD_DIM)
        qib = qi1.reshape(nb, QBLOCK, IDX_HEADS, IDX_DIM)
        wib = wi1.reshape(nb, QBLOCK, IDX_HEADS)
        starts = jnp.arange(nb) * QBLOCK
        kif = ki1.astype(jnp.float32)

        def block(args):
            qq, qx, ww, t0 = args
            s = jnp.einsum('thd,sd->ths', qx.astype(jnp.float32), kif) * (IDX_DIM ** -0.5)
            score = jnp.einsum('ths,th->ts', jax.nn.relu(s), ww.astype(jnp.float32))
            q_chunk = (t0 + jnp.arange(QBLOCK)) // CHUNK
            adm = key_chunk[None, :] <= q_chunk[:, None]
            score = jnp.where(adm, score, -jnp.inf)
            _, idx = lax.top_k(score, topk)
            valid = jnp.take_along_axis(adm, idx, axis=1)
            kg = k1[idx].astype(jnp.float32)
            vg = v1[idx].astype(jnp.float32)
            logits = jnp.einsum('thd,tkhd->thk', qq.astype(jnp.float32), kg) * (HEAD_DIM ** -0.5)
            logits = jnp.where(valid[:, None, :], logits, -jnp.inf)
            p = jax.nn.softmax(logits, axis=-1)
            o = jnp.einsum('thk,tkhd->thd', p, vg)
            return o.astype(q1.dtype)

        out = lax.map(block, (qb, qib, wib, starts))
        return out.reshape(S, ATTN_HEADS, HEAD_DIM)

    return jax.vmap(per_seq)(q, k, v, qi, ki, wi)

def setup_inputs(seed: int = 0) -> dict:
    key = jax.random.key(seed)
    ks = jax.random.split(key, 16)
    f32 = jnp.float32
    def nrm(k, shape, fan_in):
        return jax.random.normal(k, shape, f32) * (fan_in ** -0.5)
    return {
        "x": jax.random.normal(ks[0], (BATCH, SEQ, D_MODEL), f32),
        "norm1": 1.0 + 0.02 * jax.random.normal(ks[1], (DEPTH, D_MODEL), f32),
        "w_in": nrm(ks[2], (DEPTH, D_MODEL, IN_WIDTH), D_MODEL),
        "pool_w": nrm(ks[3], (DEPTH, POOL_GROUPS, POOL_GC, POOL_GC), POOL_GC),
        "pool_scale": 1.0 + 0.02 * jax.random.normal(ks[4], (DEPTH, POOL_WIDTH), f32),
        "conv_w": nrm(ks[5], (DEPTH, CONV_K, CONV_WIDTH), CONV_K),
        "q_gain": 1.0 + 0.02 * jax.random.normal(ks[6], (DEPTH, HEAD_DIM), f32),
        "k_gain": 1.0 + 0.02 * jax.random.normal(ks[7], (DEPTH, HEAD_DIM), f32),
        "w_pool_out": nrm(ks[8], (DEPTH, POOL_WIDTH, D_MODEL), POOL_WIDTH),
        "w_conv_out": nrm(ks[9], (DEPTH, CONV_WIDTH, D_MODEL), CONV_WIDTH),
        "w_attn_out": nrm(ks[10], (DEPTH, ATTN_WIDTH, D_MODEL), ATTN_WIDTH),
        "w_o": nrm(ks[11], (DEPTH, D_MODEL, D_MODEL), D_MODEL),
        "norm2": 1.0 + 0.02 * jax.random.normal(ks[12], (DEPTH, D_MODEL), f32),
        "w_ff1": nrm(ks[13], (DEPTH, D_MODEL, D_FF), D_MODEL),
        "w_ff2": nrm(ks[14], (DEPTH, D_FF, D_MODEL), D_FF),
    }

def reference(x, norm1, w_in, pool_w, pool_scale, conv_w, q_gain, k_gain,
              w_pool_out, w_conv_out, w_attn_out, w_o, norm2, w_ff1, w_ff2):
    B, S, D = x.shape
    topk = min(TOPK_MAX, S // 4)
    pts = _split_points()
    for l in range(DEPTH):
        h = _rmsnorm(x, norm1[l])
        proj = jnp.einsum('bsd,de->bse', h, w_in[l])
        (u_pool, c_b, c_c, c_x, q, k, v, qi, ki, wi, gate_logits) = jnp.split(proj, pts, axis=-1)

        a = _multiscale_pool(u_pool, pool_w[l], pool_scale[l])
        bconv = _short_conv(c_b, c_c, c_x, conv_w[l])
        q = _rmsnorm(q.reshape(B, S, ATTN_HEADS, HEAD_DIM), q_gain[l])
        k = _rmsnorm(k.reshape(B, S, ATTN_HEADS, HEAD_DIM), k_gain[l])
        v = v.reshape(B, S, ATTN_HEADS, HEAD_DIM)
        qi = qi.reshape(B, S, IDX_HEADS, IDX_DIM)
        wi = wi * (IDX_HEADS ** -0.5)
        c = _sparse_attention(q, k, v, qi, ki, wi, topk).reshape(B, S, ATTN_WIDTH)

        g = jax.nn.sigmoid(gate_logits.astype(jnp.float32)).reshape(B, S, N_BRANCH, D).astype(x.dtype)
        merged = (g[:, :, 0] * jnp.einsum('bsp,pd->bsd', a, w_pool_out[l])
                  + g[:, :, 1] * jnp.einsum('bsp,pd->bsd', bconv, w_conv_out[l])
                  + g[:, :, 2] * jnp.einsum('bsp,pd->bsd', c, w_attn_out[l]))
        x = x + jnp.einsum('bsd,de->bse', merged, w_o[l])

        h2 = _rmsnorm(x, norm2[l])
        f = jnp.square(jax.nn.relu(jnp.einsum('bsd,df->bsf', h2, w_ff1[l])))
        x = x + jnp.einsum('bsf,fd->bsd', f, w_ff2[l])
    return x


_drawn_inputs = setup_inputs


def setup_inputs(seed=0):
    import zlib

    import numpy as np

    out = dict(_drawn_inputs(seed))
    spreads = {}
    factors = {'pool_scale': 7.006, 'q_gain': 8.0, 'k_gain': 8.0, 'norm2': 3.559}
    for name, (base, spread) in spreads.items():
        noise = np.random.default_rng([zlib.crc32(name.encode()), seed]).standard_normal(out[name].shape)
        drawn = base * np.exp(spread * noise) if base else spread * noise
        out[name] = __import__('jax').numpy.asarray(drawn.astype(out[name].dtype))
    for name, factor in factors.items():
        out[name] = (out[name] * factor).astype(out[name].dtype)
    return out
```

```python
from contextlib import ExitStack

import concourse.bass as bass
from concourse import mybir

F32 = mybir.dt.float32
F32R = mybir.dt.float32r
ALU = mybir.AluOpType
ACT = mybir.ActivationFunctionType
AX_X = mybir.AxisListType.X

P = 128
COLS = 256
UK = 2
SLOTS = 4
RAWS = 4
PREFETCH = 3
EPS = 1e-6
MASKED = -1e36
EMPTY = -3.0e38

POOL_WINDOWS = (2, 4, 8, 16)
CONV_K = 3
CHUNK = 64
TOPK_MAX = 256
N_BRANCH = 3
IDX_HEADS = 8
IDX_DIM = 64
ATTN_HEADS = 8

C_G1, C_G2, C_PS, C_CW, C_QG, C_KG, C_INV = 0, 16, 32, 36, 48, 49, 50
C_ID = C_INV + len(POOL_WINDOWS) * 16
C_ONE = C_ID + P
C_N = C_ONE + P


def build(nc, xT, cst_dram, w_in, pool_w, w_po, w_co, w_ao, w_o, w_f1, w_f2, outT):
    D, S = xT.shape
    FF = w_f1.shape[1]
    KT = D // P
    TT = S // P
    TOPK = min(TOPK_MAX, S // 4)
    HD = D // 16
    PW = D // 4
    AW = ATTN_HEADS * HD
    NW = len(POOL_WINDOWS)
    assert S == 512 and TOPK == P and HD == P and KT == 16 and TT == 4

    c_pool, c_b, c_c, c_x = 0, PW, 2 * PW, 3 * PW
    c_q = 4 * PW
    c_k, c_v, c_qi = c_q + AW, c_q + 2 * AW, c_q + 3 * AW
    c_ki = c_qi + IDX_HEADS * IDX_DIM
    c_gate = c_ki + IDX_DIM + IDX_HEADS
    KIW = IDX_DIM + IDX_HEADS

    UP = KT // UK
    u_idx, p_idx = 0, 0
    u_qk, p_qk = 5 * UP, 5
    u_v, p_v = u_qk + 8 * UP, p_qk + 8
    u_att, p_att = u_v + 4 * UP, p_v + 4
    u_g, p_g = u_att + 6 * UP, p_att + 6
    G_U, G_P, G_IT = 4 * UP, 6, D // COLS
    u_o, p_o = u_g + G_IT * G_U, p_g + G_IT * G_P
    u_f, p_f = u_o + 8 * UP, p_o + 8
    CH = FF // D
    CH_U, CH_P = 16 * UP, 16
    u_end = u_f + CH * CH_U
    g_ends = (8, 10, 18, 20, 28, 32)

    ctx = ExitStack()
    with ctx:
        base = -(-nc.sbuf_base // 32) * 32

        def at(name, shape, dt, offset):
            return nc.alloc_sbuf_tensor_at(name, shape, dt, offset=base + offset)

        KB = 1024
        act_hi = at("act_hi", [P, KT, S], F32R, 0)
        act_lo = at("act_lo", [P, KT, S], F32R, 32 * KB)
        BR = 64 * KB
        br_hi = at("br_hi", [P, KT, S], F32R, BR)
        br_lo = at("br_lo", [P, KT, S], F32R, BR + 32 * KB)
        qT = at("qT", [P, ATTN_HEADS, S], F32, BR + 16 * KB)
        kT = at("kT", [P, ATTN_HEADS, S], F32, BR + 48 * KB)
        poolT = at("poolT", [P, NW, S], F32, BR + 32 * KB)
        qiT = at("qiT", [P, 4, S], F32, BR + 8 * KB)
        kiT = at("kiT", [P, S], F32, BR + 40 * KB)
        score = [at(f"score{i}", [P, P * (i + 1)], F32, BR + (42 * 1024 + o)) for i, o in ((1, 0), (2, 1024), (3, 2560))]
        M = 128 * KB
        xin = at("xin", [P, KT, S], F32, M)
        vv = at("v", [P, TT, AW], F32, M)
        work = [at(f"work{i}", [P, P * (i + 1)], F32, M + o) for i, o in ((1, 0), (2, 1024), (3, 2560))]
        PCOLS = P * (1 + 2 + 3 + 4)
        maskM = at("maskM", [P, PCOLS], F32, M + 16 * KB)
        prob = at("prob", [P, PCOLS], F32, M + 21 * KB)
        probT = at("probT", [P, PCOLS], F32, M + 26 * KB)
        trunk = at("trunk", [P, KT, S], F32, M)
        R = 160 * KB
        w_hi = at("w_hi", [P, SLOTS, UK, COLS], F32R, R)
        w_lo = at("w_lo", [P, SLOTS, UK, COLS], F32R, R + 8 * KB)
        w_raw = at("w_raw", [P, RAWS, 2 * UK, COLS], F32, R + 16 * KB)
        T = 192 * KB
        cst = at("cst", [P, C_N], F32, T)
        poolw = at("poolw", [P, NW, P], F32, T + 1504)
        st = at("st", [P, 512], F32, T + 3552)
        T = T + 5600
        sq = at("sq", [P, 2, S], F32, T)
        wiT = at("wiT", [P, S], F32, T)
        PADW = 16
        U = at("U", [P, 2, PADW + S], F32, T)
        Sa = at("Sa", [P, 2, PADW + S], F32, T + 4224)
        zz = at("zz", [P, 2, CONV_K - 1 + S], F32, T)
        cc = at("cc", [P, 2, S], F32, T + 4128)
        sg = at("sg", [P, 2, S], F32, T)
        gt = at("gt", [P, 2, S], F32, T + 4096)
        xres = at("xres", [P, 2, S], F32, T + 4096)
        dg = at("dg", [P, S], F32, T + 8224)
        r2B = at("r2B", [P, S], F32, T)
        ft = at("ft", [P, 2, S], F32, T + 2048)
        ff = at("ff", [P, 2, S], F32, T + 6144)
        ssq = at("ssq", [P, S], F32, T + 8224)

        ident = cst[:, C_ID:C_ID + P]
        ones = cst[:, C_ONE:C_ONE + P]

        rqk = st[:, 0:64]
        ms64, nt64 = st[:, 64:128], st[:, 128:192]
        gqk = st[:, 192:193]
        ws = st[:, 200:200 + TT * IDX_HEADS]
        top8 = [st[:, 240 + 8 * i:248 + 8 * i] for i in range(3)]
        need = st[:, 270:273]
        mx, rsum, nmx, rinv = st[:, 280:284], st[:, 284:288], st[:, 288:292], st[:, 292:296]
        r4, ms4, nt4 = st[:, 300:304], st[:, 304:308], st[:, 308:312]

        main = ctx.enter_context(nc.psum_tensor("main", [P, 4, S], F32))
        aux = ctx.enter_context(nc.psum_tensor("aux", [P, 4, S], F32))

        def sem(name):
            return ctx.enter_context(nc.semaphore(name))

        raw_landed = [sem(f"raw_landed{i}") for i in range(RAWS)]
        hi_ready, lo_ready, unit_done = sem("hi_ready"), sem("lo_ready"), sem("unit_done")
        set_free = [sem("set_free0"), sem("set_free1")]
        x_landed = [sem(f"x_landed{i}") for i in range(4)]
        cst_landed, poolw_landed, ki_doubled = sem("cst_landed"), sem("poolw_landed"), sem("ki_doubled")
        x_squared, x_summed = sem("x_squared"), sem("x_summed")
        sums_done, root_done, diag_ready, bcast_done = sem("sums_done"), sem("root_done"), sem("diag_ready"), sem("bcast_done")
        ms_ready = sem("ms_ready")
        h_ready, h_hi = sem("h_ready"), sem("h_hi")
        h_scaled = sem("h_scaled")
        ki_ready, qi_ready, wi_turned, ws_ready = sem("ki_ready"), sem("qi_ready"), sem("wi_turned"), sem("ws_ready")
        score_mm, relu_done, score_added = sem("score_mm"), sem("relu_done"), sem("score_added")
        pool_u, pool_diff, pool_mm, a_hi, a_lo = sem("pool_u"), sem("pool_diff"), sem("pool_mm"), sem("a_hi"), sem("a_lo")
        qk_ready, qk_squared, v_ready = sem("qk_ready"), sem("qk_squared"), sem("v_ready")
        k_ready = sem("k_ready")
        masks_ready = sem("masks_ready")
        logits_mm, max_ready, exp_done, prob_ready = sem("logits_mm"), sem("max_ready"), sem("exp_done"), sem("prob_ready")
        turn_mm, turned_act, turned_dve, pv_mm, c_hi, c_lo = (
            sem("turn_mm"), sem("turned_act"), sem("turned_dve"), sem("pv_mm"), sem("c_hi"), sem("c_lo"))
        cc_ready, b_ready, b_hi, b_lo = sem("cc_ready"), sem("b_ready"), sem("b_hi"), sem("b_lo")
        sig_done, gate_used = sem("sig_done"), sem("gate_used")
        m_ready, m_hi = sem("m_ready"), sem("m_hi")
        xres_landed = sem("xres_landed")
        x2_ready, x2_hi, x2_squared, x2_added, x2_lo = (
            sem("x2_ready"), sem("x2_hi"), sem("x2_squared"), sem("x2_added"), sem("x2_lo"))
        r2_ready = sem("r2_ready")
        f_ready, f_hi, f_lo = sem("f_ready"), sem("f_hi"), sem("f_lo")
        y_ready, out_written = sem("y_ready"), sem("out_written")
        dve_chain, pads_ready, merged = sem("dve_chain"), sem("pads_ready"), sem("merged")
        topk_done, stats_ready, f_scaled = sem("topk_done"), sem("stats_ready"), sem("f_scaled")

        class Chain:

            def __init__(self, eng, s):
                self.eng, self.sem, self.n = eng, s, 0

            def step(self, ins):
                ins.then_inc(self.sem, 1)
                self.n += 1

            def wait(self):
                self.eng.wait_ge(self.sem, self.n)

        def wait_apart(eng, s, value):
            value = eng.snap(value)
            eng.wait_ge(cst_landed, 16)
            eng.wait_ge(s, value)


        def split_hi(act, g, j, width=COLS):
            act.wait_ge(raw_landed[(j // 2) % RAWS], raw_count(g, j))
            if not isinstance(g, int) or g >= SLOTS:
                act.wait_ge(unit_done, g - SLOTS + 1)
            act.activation(w_hi[:, j % SLOTS, :, 0:width],
                           w_raw[:, (j // 2) % RAWS, UK * (j % 2):UK * (j % 2) + UK, 0:width],
                           ACT.Copy).then_inc(hi_ready, 1)

        def split_lo(dve, g, j, width=COLS):
            dve.wait_ge(hi_ready, g + 1)
            dve.tensor_tensor(w_lo[:, j % SLOTS, :, 0:width],
                              w_raw[:, (j // 2) % RAWS, UK * (j % 2):UK * (j % 2) + UK, 0:width],
                              w_hi[:, j % SLOTS, :, 0:width].bitcast(F32), ALU.subtract).then_inc(lo_ready, 1)

        def raw_count(g, j):
            if isinstance(g, int):
                return 16 * (g // 8 + 1)
            return (g - j % 8) * 2 + 16

        def split_any(split, eng, g, j):
            split(eng, g, j, KIW if isinstance(g, int) and g < UP else COLS)

        def unit(pe, g, j, kt0, last_kt, bank, hi, lo, width=COLS):
            pe.wait_ge(lo_ready, g + 1)
            for k in range(UK):
                kt = kt0 + k
                for m in range(-(-width // P)):
                    c0, c1 = m * P, min(width, m * P + P)
                    out = main[0:c1 - c0, bank + m, :]
                    wh, wl = w_hi[:, j % SLOTS, k, c0:c1], w_lo[:, j % SLOTS, k, c0:c1]
                    pe.matmul(out, wh, hi[:, kt, :], start=(kt == last_kt[0]), stop=False)
                    pe.matmul(out, wh, lo[:, kt, :], start=False, stop=False)
                    mm = pe.matmul(out, wl, hi[:, kt, :], start=False, stop=(kt == last_kt[1]))
            mm.then_inc(unit_done, 1)

        def wait_set(pe, p, parity, n=None):
            if n is None:
                n = p // 2
            if not isinstance(n, int) or n >= 1:
                pe.wait_ge(set_free[parity], n)

        def token_sums(pe, square, column0, bank):
            for t in range(TT):
                mm = pe.matmul(aux[:, bank, column0 + t:column0 + t + 1], square[:, t * P:(t + 1) * P],
                               ones[:, 0:1], start=True, stop=True)
            return mm

        def newton(dve, chain, r, ms, tmp, out):
            chain.step(dve.tensor_tensor(tmp, r, r, ALU.mult))
            chain.wait()
            chain.step(dve.tensor_tensor(tmp, tmp, ms, ALU.mult))
            chain.wait()
            chain.step(dve.tensor_scalar(tmp, tmp, -0.5, 1.5, ALU.mult, ALU.add))
            chain.wait()
            return dve.tensor_tensor(out, r, tmp, ALU.mult)

        def diagonals(dve, r, column0, dg):
            for t in range(TT):
                ins = dve.tensor_scalar(dg[:, t * P:(t + 1) * P], ident, r[:, column0 + t:column0 + t + 1],
                                        None, ALU.mult)
            ins.then_inc(diag_ready, 1)

        block = ctx.enter_context(nc.Block())

        @block.sync
        def _(sp):
            for i in range(4):
                sp.dma_start(xin[:, 4 * i:4 * i + 4, :],
                             xT[4 * i * P:(4 * i + 4) * P, :].rearrange("(t p) s -> p t s", p=P)
                             ).then_inc(x_landed[i], 16)

            def load(L, slot, w, row0, col0, width=COLS):
                if not isinstance(L, int) or L >= RAWS:
                    sp.wait_ge(lo_ready, (L - RAWS) * 2 + 2)
                rows = w[bass.ds(row0, 2 * UK * P), bass.ds(col0, width)].rearrange("(t p) c -> p t c", p=P)
                sp.dma_start(w_raw[:, slot, :, 0:width], rows).then_inc(raw_landed[slot], 16)

            LP = UP // 2
            for i, (col, width) in enumerate(((c_ki, KIW), (c_qi, COLS), (c_qi + COLS, COLS),
                                              (c_pool, COLS), (c_pool + COLS, COLS))):
                for n in range(LP):
                    load(i * LP + n, n % RAWS, w_in, n * 2 * UK * P, col, width)
            with sp.Fori(0, 8) as i:
                for n in range(LP):
                    load(i * LP + (u_qk // 2 + n), n % RAWS, w_in, n * 2 * UK * P, i * COLS + c_q)
            with sp.Fori(0, 4) as i:
                for n in range(LP):
                    load(i * LP + (u_v // 2 + n), n % RAWS, w_in, n * 2 * UK * P, i * COLS + c_v)
            for i, col in enumerate((c_c, c_x, c_b, c_c + COLS, c_x + COLS, c_b + COLS)):
                for n in range(LP):
                    load(u_att // 2 + i * LP + n, n % RAWS, w_in, n * 2 * UK * P, col)
            with sp.Fori(1, G_IT + 1) as next_i:
                i = next_i - 1
                n_load = 0
                for b, (w, loads) in enumerate(((w_po, 1), (w_co, 1), (w_ao, 2))):
                    for n in range(LP):
                        load(i * (G_U // 2) + (u_g // 2 + n_load), n_load % RAWS, w_in, n * 2 * UK * P,
                             i * COLS + (c_gate + b * D))
                        n_load += 1
                    for n in range(loads):
                        load(i * (G_U // 2) + (u_g // 2 + n_load), n_load % RAWS, w, n * 2 * UK * P,
                             next_i * COLS - COLS)
                        n_load += 1
            with sp.Fori(0, 8) as i:
                for n in range(LP):
                    load(i * LP + (u_o // 2 + n), n % RAWS, w_o, n * 2 * UK * P, i * COLS)
            with sp.Fori(0, CH) as c:
                with sp.Fori(0, 8) as i:
                    for n in range(LP):
                        load(c * (CH_U // 2) + i * LP + (u_f // 2 + n), n % RAWS, w_f1, n * 2 * UK * P,
                             c * D + i * COLS)
                with sp.Fori(0, 8) as i:
                    for n in range(LP):
                        load(c * (CH_U // 2) + i * LP + (u_f // 2 + CH_U // 4 + n), n % RAWS, w_f2,
                             c * D + n * 2 * UK * P, i * COLS)

        @block.tensor
        def _(pe):
            H = (0, KT - 1)
            pe.wait_ge(cst_landed, 16)
            pe.wait_ge(x_summed, KT)
            token_sums(pe, dg, 0, 3).then_inc(sums_done, 1)
            pe.wait_ge(diag_ready, 1)
            pe.matmul(aux[:, 0, :], ones, dg[:, :], start=True, stop=True).then_inc(bcast_done, 1)

            for j in range(UP):
                pe.wait_ge(h_ready, 2 * j + 2)
                unit(pe, j, j, 2 * j, H, 0, act_hi, act_lo, KIW)

            def score_product(n):
                i, h = 1 + n // 8, n % 8
                if n == 0:
                    pe.wait_ge(ki_doubled, 16)
                    pe.wait_ge(qi_ready, 4)
                if n >= 2:
                    pe.wait_ge(relu_done, n - 1)
                lo_p = IDX_DIM * (h % 2)
                pe.matmul(aux[:, n % 2, 0:P * (i + 1)], qiT[lo_p:lo_p + IDX_DIM, h // 2, i * P:(i + 1) * P],
                          kiT[lo_p:lo_p + IDX_DIM, 0:P * (i + 1)], start=True, stop=True).then_inc(score_mm, 1)

            for p in range(1, 5):
                wait_set(pe, p, p % 2)
                for j in range(UP):
                    g = p * UP + j
                    if p == 1 and j == 4:
                        pe.wait_ge(ki_ready, 2)
                        for t in range(TT):
                            mm = pe.transpose(aux[:, 3, 16 + 8 * t:24 + 8 * t], wiT[IDX_DIM:KIW, t * P:(t + 1) * P],
                                              cst[IDX_DIM:KIW, C_ID + IDX_DIM:C_ID + KIW])
                        mm.then_inc(wi_turned, 1)
                    s = (p - 3) * UP + j - 3
                    if p >= 3 and 0 <= s < 12:
                        score_product(2 * s)
                        score_product(2 * s + 1)
                    unit(pe, g, j, 2 * j, H, 2 * (p % 2), act_hi, act_lo)

            def pass_pair(u0, hi, lo, p0, n0, n1):
                for q in range(2):
                    parity = (p0 + q) % 2
                    wait_set(pe, None, parity, (n0, n1)[q])
                    for j in range(UP):
                        unit(pe, u0 + (q * UP + j), j, 2 * j, H, 2 * parity, hi, lo)

            with pe.Fori(0, 4) as i:
                pass_pair(i * (2 * UP) + u_qk, act_hi, act_lo, p_qk, i + p_qk // 2, i + (p_qk + 1) // 2)

            def k_spread(h):
                pe.wait_ge(diag_ready, 2 + h)
                if h >= 1:
                    pe.wait_ge(turned_act, 2 * h)
                else:
                    pe.wait_ge(a_lo, NW)
                pe.matmul(aux[:, 0, :], ones, dg[:, :], start=True, stop=True).then_inc(bcast_done, 1)

            for q in range(4):
                p = p_v + q
                wait_set(pe, p, p % 2)
                for j in range(UP):
                    g = u_v + q * UP + j
                    n = q * UP + j
                    if n < 16:
                        pe.wait_ge(qk_squared, n + 1)
                        if n == 0:
                            pe.wait_ge(ws_ready, 1)
                        token_sums(pe, sq[:, n % 2], 4 * n, 3).then_inc(sums_done, 1)
                    if 16 <= n < 16 + NW:
                        gr = n - 16
                        if gr == 0:
                            pe.wait_ge(relu_done, 24)
                            pe.wait_ge(poolw_landed, 16)
                            pe.wait_ge(pool_diff, NW)
                        if gr >= 2:
                            pe.wait_ge(a_lo, gr - 1)
                        pe.matmul(aux[:, gr % 2, :], poolw[:, gr, :], poolT[:, gr, :], start=True,
                                  stop=True).then_inc(pool_mm, 1)
                    if n == 4 * UP - 1:
                        k_spread(0)
                    pe.wait_ge(lo_ready, g + 1)
                    for k in range(UK):
                        kt = 2 * j + k
                        for t in range(TT):
                            out = main[:, 2 * (p % 2) + t // 2, (t % 2) * COLS:(t % 2 + 1) * COLS]
                            th, tl = act_hi[:, kt, t * P:(t + 1) * P], act_lo[:, kt, t * P:(t + 1) * P]
                            wh, wl = w_hi[:, j % SLOTS, k, :], w_lo[:, j % SLOTS, k, :]
                            pe.matmul(out, th, wh, start=(kt == 0 and t % 2 == 0), stop=False, skip_group_check=True)
                            pe.matmul(out, th, wl, start=False, stop=False, skip_group_check=True)
                            mm = pe.matmul(out, tl, wh, start=False, stop=(kt == KT - 1), skip_group_check=True)
                    mm.then_inc(unit_done, 1)

            logit_at = {3: (0, 0), 2: (1, 0), 0: (1, 3 * P), 1: (2, 0)}

            def logits(h):
                pe.wait_ge(k_ready, h + 1)
                if h >= 1:
                    pe.wait_ge(turned_act, 2 * h)
                    pe.wait_ge(turned_dve, h)
                for i in (3, 2, 1, 0):
                    bank, c0 = logit_at[i]
                    pe.matmul(aux[:, bank, c0:c0 + P * (i + 1)], qT[:, h, i * P:(i + 1) * P],
                              kT[:, h, 0:P * (i + 1)], start=True, stop=True).then_inc(logits_mm, 1)

            prob_at = {i: P * i * (i + 1) // 2 for i in range(TT)}
            turn_at = {0: (0, 0), 1: (1, 0), 2: (2, 0), 3: (1, 3 * P)}

            def turns(h):
                pe.wait_ge(prob_ready, h + 1)
                for kb in range(TT):
                    bank, c0 = turn_at[kb]
                    for i in range(kb, TT):
                        c = prob_at[i] + kb * P
                        mm = pe.transpose(aux[:, bank, c0 + (i - kb) * P:c0 + (i - kb + 1) * P],
                                          prob[:, c:c + P], ident)
                mm.then_inc(turn_mm, 1)

            probT_at = {0: 0, 1: 4 * P, 3: 7 * P, 2: 8 * P}

            def pv(h):
                pe.wait_ge(turned_act, 2 * h + 2)
                pe.wait_ge(turned_dve, h + 1)
                if h == 0:
                    pe.wait_ge(v_ready, 8)
                else:
                    pe.wait_ge(c_lo, h)
                for kb in range(TT):
                    n = (TT - kb) * P
                    mm = pe.matmul(aux[:, 3, kb * P:S], vv[:, kb, h * HD:(h + 1) * HD],
                                   probT[:, probT_at[kb]:probT_at[kb] + n], start=(kb == 0), stop=(kb == TT - 1),
                                   skip_group_check=True)
                mm.then_inc(pv_mm, 1)

            for q in range(6):
                p = p_att + q
                wait_set(pe, p, p % 2)
                for j in range(UP):
                    n = q * UP + j
                    h, s = n // 6, n % 6
                    if s == 1:
                        logits(h)
                    elif s == 4:
                        turns(h)
                    elif s == 5:
                        pv(h)
                        if h + 1 < ATTN_HEADS:
                            k_spread(h + 1)
                    unit(pe, u_att + n, j, 2 * j, H, 2 * (p % 2), act_hi, act_lo)

            with pe.Fori(0, G_IT) as i:
                j = 0
                for b, (t0, units) in enumerate(((0, 2), (4, 2), (8, 4))):
                    for gate in (True, False):
                        q = 2 * b + (not gate)
                        p = p_g + q
                        wait_set(pe, None, p % 2, i * (G_P // 2) + p // 2)
                        if not gate:
                            if b == 0:
                                pe.wait_ge(a_lo, NW)
                            elif b == 1:
                                pe.wait_ge(b_lo, 4)
                            else:
                                pe.wait_ge(c_lo, ATTN_HEADS)
                        for n in range(UP if gate else units):
                            g = i * G_U + (u_g + j)
                            if gate:
                                unit(pe, g, j, 2 * n, H, 2 * (p % 2), act_hi, act_lo)
                            else:
                                unit(pe, g, j, t0 + 2 * n, (t0, t0 + 2 * units - 1), 2 * (p % 2), br_hi, br_lo)
                            j += 1

            with pe.Fori(0, 4) as i:
                for q in range(2):
                    p = p_o + q
                    wait_set(pe, None, p % 2, i + p // 2)
                    for j in range(UP):
                        if q == 0:
                            pe.wait_ge(m_ready, 2 * j + 2)
                        unit(pe, i * (2 * UP) + (u_o + q * UP + j), j, 2 * j, H, 2 * (p % 2), act_hi, act_lo)

            pe.wait_ge(x2_added, KT + 1)
            token_sums(pe, ssq, 0, 3).then_inc(sums_done, 1)
            pe.wait_ge(diag_ready, 2 + ATTN_HEADS)
            pe.matmul(aux[:, 0, :], ones, ft[:, 1, :], start=True, stop=True).then_inc(bcast_done, 1)

            pe.wait_ge(x2_lo, KT)
            with pe.Fori(0, CH) as c:
                with pe.Fori(0, 4) as i:
                    g0 = c * CH_U + i * (2 * UP) + u_f
                    n = c * (CH_P // 2) + i
                    pass_pair(g0, br_hi, br_lo, p_f, n + p_f // 2, n + (p_f + 1) // 2)
                with pe.Fori(0, 4) as i:
                    for q in range(2):
                        p = p_f + q
                        wait_set(pe, None, p % 2, c * (CH_P // 2) + i + (4 + p // 2))
                        for j in range(UP):
                            if q == 0:
                                pe.wait_ge(f_lo, c * KT + (2 * j + 2))
                            unit(pe, c * CH_U + i * (2 * UP) + (u_f + 8 * UP + q * UP + j), j, 2 * j, H,
                                 2 * (p % 2), act_hi, act_lo)

        def v_evict(act, q):
            p = p_v + q
            act.wait_ge(unit_done, u_v + (q + 1) * UP)
            if q == 0:
                act.wait_ge(topk_done, 1)
            for b in range(2):
                act.activation(vv[:, 2 * b:2 * b + 2, q * COLS:(q + 1) * COLS],
                               main[:, 2 * (p % 2) + b, :].rearrange("p (t c) -> p t c", t=2),
                               ACT.Copy).then_inc(v_ready, 1)
            act.wait_ge(v_ready, 2 * q + 2)
            act.sem_inc(set_free[p % 2], 1)

        @block.scalar
        def _(act):
            act.dma_start(cst[:], cst_dram).then_inc(cst_landed, 16)
            act.dma_start(poolw[:], pool_w.rearrange("g c d -> c g d")).then_inc(poolw_landed, 16)

            for kt in range(KT):
                if kt % 4 == 0:
                    act.wait_ge(x_landed[kt // 4], 16)
                if kt >= 2:
                    act.wait_ge(x_summed, kt - 1)
                act.activation(sq[:, kt % 2], xin[:, kt, :], ACT.Square).then_inc(x_squared, 1)
            act.wait_ge(ms_ready, 1)
            act.activation(r4, ms4, ACT.Sqrt).then_inc(root_done, 1)
            for g in range(PREFETCH):
                split_any(split_hi, act, g, g)
            for kt in range(KT):
                act.wait_ge(h_scaled, kt + 1)
                act.activation(act_hi[:, kt, :], xin[:, kt, :], ACT.Copy).then_inc(h_hi, 1)

            def relu_scores(n):
                i = 1 + n // 8
                act.wait_ge(score_mm, n + 1)
                if n >= 2:
                    act.wait_ge(score_added, n - 1)
                act.activation(prob[:, (n % 2) * S:(n % 2) * S + P * (i + 1)], aux[:, n % 2, 0:P * (i + 1)],
                               ACT.Relu).then_inc(relu_done, 1)

            def pool_copy(m, bank):
                if m >= 2:
                    act.wait_ge(pool_diff, m - 1)
                act.activation(U[:, m % 2, PADW:], bank, ACT.Copy).then_inc(pool_u, 1)

            for g in range(u_idx, u_qk):
                if g == UP:
                    act.wait_ge(unit_done, UP)
                    act.activation(kiT[0:IDX_DIM, :], main[0:IDX_DIM, 0, :], ACT.Copy).then_inc(ki_ready, 1)
                    act.activation(wiT[IDX_DIM:KIW, :], main[IDX_DIM:KIW, 0, :], ACT.Copy).then_inc(ki_ready, 1)
                    act.wait_ge(ki_ready, 2)
                    act.dma_start(kiT[IDX_DIM:2 * IDX_DIM, :], kiT[0:IDX_DIM, :]).then_inc(ki_doubled, 16)
                    act.sem_inc(set_free[0], 1)
                if g in (2 * UP, 3 * UP):
                    p = g // UP - 1
                    act.wait_ge(unit_done, g)
                    for m in range(2):
                        act.activation(qiT[:, 2 * (p - 1) + m, :], main[:, 2 * (p % 2) + m, :],
                                       ACT.Copy).then_inc(qi_ready, 1)
                    act.wait_ge(qi_ready, 2 * p)
                    act.sem_inc(set_free[p % 2], 1)
                if g == 4 * UP:
                    act.wait_ge(unit_done, g)
                    act.wait_ge(pads_ready, 1)
                    for m in range(2):
                        pool_copy(m, main[:, 2 + m, :])
                    act.wait_ge(pool_u, 2)
                    act.sem_inc(set_free[1], 1)
                split_any(split_hi, act, g + PREFETCH, g + PREFETCH)
                s = g - 3 * UP - 3
                if 0 <= s < 12:
                    relu_scores(2 * s)
                    relu_scores(2 * s + 1)
            act.wait_ge(unit_done, u_qk)
            for m in range(2, 4):
                pool_copy(m, main[:, m - 2, :])
            act.wait_ge(pool_u, 4)
            act.sem_inc(set_free[0], 1)

            for part, dst in enumerate((qT, kT)):
                with act.Fori(0, 2) as i:
                    for j in range(2 * UP):
                        split_hi(act, i * (2 * UP) + (u_qk + part * 4 * UP + j + PREFETCH), j + PREFETCH)
                        if j % UP == UP - 1:
                            q = j // UP
                            parity = (p_qk + q) % 2
                            wait_apart(act, unit_done, i * (2 * UP) + (u_qk + part * 4 * UP + j + 1))
                            for m in range(2):
                                act.activation(dst[:, bass.ds(i * 4 + (2 * q + m), 1), :],
                                               main[:, 2 * parity + m:2 * parity + m + 1, :],
                                               ACT.Copy).then_inc(qk_ready, 1)
                            act.wait_ge(qk_ready, i * 4 + (8 * part + 2 * q + 2))
                            act.sem_inc(set_free[parity], 1)

            for n in range(4 * UP):
                if n % UP == 0 and n:
                    v_evict(act, n // UP - 1)
                split_hi(act, u_v + n + PREFETCH, n + PREFETCH)
                if n < 16:
                    src = qT if n < 8 else kT
                    if n == 0:
                        act.wait_ge(pool_diff, NW)
                    if n >= 2:
                        act.wait_ge(sums_done, 1 + n - 1)
                    act.activation(sq[:, n % 2], src[:, n % 8, :], ACT.Square).then_inc(qk_squared, 1)
                if n == 18:
                    act.wait_ge(ms_ready, 2)
                    act.activation(rqk, ms64, ACT.Sqrt).then_inc(root_done, 1)
                if 17 <= n < 17 + NW:
                    gr = n - 17
                    act.wait_ge(pool_mm, gr + 1)
                    act.activation(br_hi[:, gr, :], aux[:, gr % 2, :], ACT.Copy,
                                   scale=cst[:, C_PS + gr:C_PS + gr + 1]).then_inc(a_hi, 1)
            v_evict(act, 3)

            logit_at = {3: (0, 0), 2: (1, 0), 0: (1, 3 * P), 1: (2, 0)}
            prob_at = {i: P * i * (i + 1) // 2 for i in range(TT)}
            for n in range(6 * UP + 1):
                h, s = n // 6, n % 6
                if n % UP == 0 and n:
                    q = n // UP - 1
                    p = p_att + q
                    if q % 3 == 0:
                        act.wait_ge(unit_done, u_att + n)
                        if q:
                            act.wait_ge(b_lo, 2)
                        for m in range(2):
                            act.activation(cc[:, m], main[:, 2 * (p % 2) + m, :], ACT.Copy).then_inc(cc_ready, 1)
                        act.wait_ge(cc_ready, 2 * (q // 3) + 2)
                        act.sem_inc(set_free[p % 2], 1)
                    elif q % 3 == 2:
                        for m in range(2):
                            act.wait_ge(b_ready, 2 * (q // 3) + m + 1)
                            act.activation(br_hi[:, 4 + 2 * (q // 3) + m, :], cc[:, m], ACT.Copy).then_inc(b_hi, 1)
                if s == 0 and n:
                    act.wait_ge(pv_mm, h)
                    act.activation(br_hi[:, 8 + h - 1, :], aux[:, 3, :], ACT.Copy).then_inc(c_hi, 1)
                if n == 6 * UP:
                    break
                split_hi(act, u_att + n + PREFETCH, n + PREFETCH)
                if s == 2:
                    act.wait_ge(max_ready, h + 1)
                    for i in (3, 2, 1, 0):
                        c = prob_at[i]
                        act.activation(prob[:, c:c + P * (i + 1)], prob[:, c:c + P * (i + 1)], ACT.Exp,
                                       bias=nmx[:, i:i + 1], accum_out=rsum[:, i:i + 1]).then_inc(exp_done, 1)
                if s == 4:
                    act.wait_ge(turn_mm, h + 1)
                    if h:
                        act.wait_ge(pv_mm, h)
                    for b in range(2):
                        act.activation(probT[:, b * S:(b + 1) * S], aux[:, b, :], ACT.Copy).then_inc(turned_act, 1)

            with act.Fori(0, G_IT) as i:
                n_gate = 0
                for j in range(G_U + 1):
                    if j in g_ends and g_ends.index(j) % 2 == 0:
                        q = g_ends.index(j)
                        parity = (p_g + q) % 2
                        act.wait_ge(unit_done, i * G_U + (u_g + j))
                        act.wait_ge(gate_used, i * 6 + (2 * n_gate + 1))
                        for m in range(2):
                            act.activation(sg[:, m], main[:, 2 * parity + m, :], ACT.Sigmoid).then_inc(sig_done, 1)
                        act.wait_ge(sig_done, i * 6 + (2 * n_gate + 2))
                        act.sem_inc(set_free[parity], 1)
                        n_gate += 1
                    if j < G_U:
                        split_hi(act, i * G_U + (u_g + j + PREFETCH), j + PREFETCH)

            act.wait_ge(unit_done, u_o - 4)
            act.wait_ge(merged, G_IT * 4)
            for kt in range(KT):
                act.activation(act_hi[:, kt, :], trunk[:, kt, :], ACT.Copy).then_inc(m_hi, 1)

            for q in range(8):
                act.dma_start(xres[:], xT[q * COLS:(q + 1) * COLS, :].rearrange("(m p) s -> p m s", p=P)
                              ).then_inc(xres_landed, 16)
                for j in range(UP):
                    g = u_o + q * UP + j + PREFETCH
                    split_hi(act, g, g)
                act.wait_ge(x2_ready, 2 * q + 2)
                for m in range(2):
                    t = 2 * q + m
                    act.activation(br_hi[:, t, :], trunk[:, t, :], ACT.Copy,
                                   scale=cst[:, C_G2 + t:C_G2 + t + 1]).then_inc(x2_hi, 1)
                    act.wait_ge(x2_added, t + 1)
                    act.activation(sq[:, 0, :], trunk[:, t, :], ACT.Square).then_inc(x2_squared, 1)
            act.wait_ge(ms_ready, 3)
            act.activation(r4, ms4, ACT.Sqrt).then_inc(root_done, 1)
            act.wait_ge(bcast_done, 2 + ATTN_HEADS)
            act.activation(r2B[:, :], aux[:, 0, :], ACT.Copy).then_inc(r2_ready, 1)

            def hidden_chunk(c, last):
                with act.Fori(0, 4) as i:
                    for j in range(2 * UP):
                        split_hi(act, c * CH_U + i * (2 * UP) + (u_f + j + PREFETCH), j + PREFETCH)
                        if j % UP == UP - 1:
                            for m in range(2):
                                t = i * 4 + (2 * (j // UP) + m)
                                wait_apart(act, f_ready, c * KT + t + 1)
                                act.activation(act_hi[:, bass.ds(t, 1), :], ff[:, m:m + 1, :],
                                               ACT.Copy).then_inc(f_hi, 1)
                with act.Fori(0, 7) as i:
                    for j in range(UP):
                        split_hi(act, c * CH_U + i * UP + (u_f + 8 * UP + j + PREFETCH), j + PREFETCH)
                for j in range(UP - PREFETCH if last else UP):
                    split_hi(act, c * CH_U + (u_f + 15 * UP + j + PREFETCH), j + PREFETCH)

            with act.Fori(0, CH - 1) as c:
                hidden_chunk(c, False)
            hidden_chunk(CH - 1, True)

        @block.vector
        def _(dve):
            chain = Chain(dve, dve_chain)

            for kt in range(KT):
                dve.wait_ge(x_squared, kt + 1)
                if kt == 0:
                    dve.tensor_copy(dg[:, :], sq[:, 0]).then_inc(x_summed, 1)
                else:
                    dve.wait_ge(x_summed, kt)
                    dve.tensor_tensor(dg[:, :], dg[:, :], sq[:, kt % 2], ALU.add).then_inc(x_summed, 1)

            def scale_of_tokens(n_sums, n_root, r, ms, tmp, source, width):
                dve.wait_ge(sums_done, n_sums)
                dve.tensor_scalar(ms, source, 1.0 / width, EPS, ALU.mult, ALU.add).then_inc(ms_ready, 1)
                dve.wait_ge(root_done, n_root)
                chain.step(dve.reciprocal(r, r))
                chain.wait()
                chain.step(newton(dve, chain, r, ms, tmp, r))
                chain.wait()

            scale_of_tokens(1, 1, r4, ms4, nt4, aux[:, 3, 0:TT], D)
            diagonals(dve, r4, 0, dg)
            for g in range(PREFETCH):
                split_any(split_lo, dve, g, g)
            dve.wait_ge(bcast_done, 1)
            for kt in range(KT + 1):
                if kt < KT:
                    dve.scalar_tensor_tensor(xin[:, kt, :], xin[:, kt, :], cst[:, C_G1 + kt:C_G1 + kt + 1],
                                             aux[:, 0, :], ALU.mult, ALU.mult).then_inc(h_scaled, 1)
                if kt:
                    dve.wait_ge(h_hi, kt)
                    dve.tensor_tensor(act_lo[:, kt - 1, :], xin[:, kt - 1, :], act_hi[:, kt - 1, :].bitcast(F32),
                                      ALU.subtract).then_inc(h_ready, 1)

            def add_score(n):
                i, h = 1 + n // 8, n % 8
                dve.wait_ge(relu_done, n + 1)
                if n == 0:
                    dve.wait_ge(ws_ready, 1)
                src = prob[:, (n % 2) * S:(n % 2) * S + P * (i + 1)]
                w = ws[:, i * IDX_HEADS + h:i * IDX_HEADS + h + 1]
                if h == 0:
                    dve.tensor_scalar(score[i - 1][:], src, w, None, ALU.mult).then_inc(score_added, 1)
                else:
                    dve.wait_ge(score_added, n)
                    dve.scalar_tensor_tensor(score[i - 1][:], src, w, score[i - 1][:], ALU.mult,
                                             ALU.add).then_inc(score_added, 1)

            def pool_group(gr):
                m, w = gr % 2, POOL_WINDOWS[gr]
                dve.wait_ge(pool_u, gr + 1)
                cur = U[:, m]
                for s in range(gr + 1):
                    nxt = Sa[:, s % 2]
                    chain.step(dve.tensor_tensor(nxt[:, PADW:], cur[:, PADW:],
                                                 cur[:, PADW - (1 << s):PADW - (1 << s) + S], ALU.add))
                    chain.wait()
                    cur = nxt
                chain.step(dve.tensor_tensor(st[:, 320:336], cur[:, PADW:PADW + 16],
                                             cst[:, C_INV + 16 * gr:C_INV + 16 * gr + 16], ALU.mult))
                chain.step(dve.scalar_tensor_tensor(poolT[:, gr, 16:], cur[:, PADW + 16:], 1.0 / w,
                                                    U[:, m, PADW + 16:], ALU.mult, ALU.subtract))
                chain.wait()
                dve.tensor_tensor(poolT[:, gr, 0:16], st[:, 320:336], U[:, m, PADW:PADW + 16],
                                  ALU.subtract).then_inc(pool_diff, 1)

            for g in range(u_idx, u_qk):
                if g == 4 * UP:
                    pool_group(0)
                    pool_group(1)
                split_any(split_lo, dve, g + PREFETCH, g + PREFETCH)
                if g == UP + 6:
                    dve.wait_ge(wi_turned, 1)
                    dve.tensor_scalar(ws, aux[:, 3, 16:16 + TT * IDX_HEADS], IDX_HEADS ** -0.5, IDX_DIM ** -0.5,
                                      ALU.mult, ALU.mult).then_inc(ws_ready, 1)
                    dve.memset(U[:, :, 0:PADW], 0.0)
                    dve.memset(Sa[:, :, 0:PADW], 0.0).then_inc(pads_ready, 1)
                    dve.wait_ge(pads_ready, 1)
                s = g - 3 * UP - 3
                if 0 <= s < 12:
                    add_score(2 * s)
                    add_score(2 * s + 1)
            dve.wait_ge(score_added, 24)
            for i in (1, 2, 3):
                chain.step(dve.memset(score[i - 1][0:CHUNK, i * P + CHUNK:(i + 1) * P], EMPTY))
            chain.wait()
            for i in (1, 2, 3):
                chain.step(dve.tensor_copy(work[i - 1][:], score[i - 1][:]))
            chain.wait()
            pool_group(2)
            pool_group(3)

            for n in range(8 * UP):
                split_lo(dve, u_qk + n + PREFETCH, n + PREFETCH)
                if n % UP < 6:
                    t = n % UP % 3
                    chain.step(dve.max(top8[t], work[t][:]))
                    chain.wait()
                    chain.step(dve.match_replace(work[t][:], top8[t], work[t][:], EMPTY))
                    chain.wait()

            prob_at = {i: P * i * (i + 1) // 2 for i in range(TT)}

            def mask(t):
                i = t + 1
                n = P * (i + 1)
                dst = maskM[:, prob_at[i]:prob_at[i] + n]
                kth = top8[t][:, 7:8]
                above, equal, rank = dst, work[t][:], prob[:, 0:n]
                chain.step(dve.tensor_scalar(above, score[t][:], kth, None, ALU.is_gt, ALU.add,
                                             accum_out=need[:, t:t + 1]))
                chain.step(dve.tensor_scalar(equal, score[t][:], kth, None, ALU.is_equal))
                chain.wait()
                chain.step(dve.tensor_scalar(need[:, t:t + 1], need[:, t:t + 1], -1.0, float(TOPK), ALU.mult, ALU.add))
                chain.step(dve.tensor_tensor_scan(rank, equal, equal, 0.0, ALU.add, ALU.max))
                chain.wait()
                chain.step(dve.scalar_tensor_tensor(rank, rank, need[:, t:t + 1], equal, ALU.is_le, ALU.mult))
                chain.wait()
                chain.step(dve.tensor_tensor(dst, dst, rank, ALU.add))
                chain.wait()
                return dve.tensor_scalar(dst, dst, -1.0, -MASKED, ALU.add, ALU.mult)

            for n in range(4 * UP):
                split_lo(dve, u_v + n + PREFETCH, n + PREFETCH)
                if n in (0, 2, 4):
                    ins = mask(n // 2)
                    if n == 4:
                        ins.then_inc(topk_done, 1)
                    else:
                        chain.step(ins)
                if n == 6:
                    chain.step(dve.memset(maskM[:, 0:P], 0.0))
                    chain.wait()
                    dve.memset(maskM[0:CHUNK, CHUNK:P], MASKED).then_inc(masks_ready, 1)
                if 17 <= n < 17 + NW:
                    gr = n - 17
                    dve.wait_ge(a_hi, gr + 1)
                    dve.scalar_tensor_tensor(br_lo[:, gr, :], aux[:, gr % 2, :], cst[:, C_PS + gr:C_PS + gr + 1],
                                             br_hi[:, gr, :].bitcast(F32), ALU.mult, ALU.subtract).then_inc(a_lo, 1)
                if n == 17:
                    dve.wait_ge(sums_done, 17)
                    dve.tensor_scalar(ms64, aux[:, 3, 0:64], 1.0 / HD, EPS, ALU.mult, ALU.add).then_inc(ms_ready, 1)
                if n == 22:
                    dve.wait_ge(root_done, 2)
                    chain.step(dve.reciprocal(rqk, rqk))
                    chain.wait()
                    chain.step(newton(dve, chain, rqk, ms64, nt64, rqk))
                    chain.step(dve.tensor_tensor(gqk, cst[:, C_QG:C_QG + 1], cst[:, C_KG:C_KG + 1], ALU.mult))
                    chain.wait()
                    chain.step(dve.tensor_scalar(rqk[:, 0:32], rqk[:, 0:32], HD ** -0.5, None, ALU.mult))
                    chain.wait()
                if n == 24:
                    diagonals(dve, rqk, 32, dg)

            logit_at = {3: (0, 0), 2: (1, 0), 0: (1, 3 * P), 1: (2, 0)}
            for n in range(6 * UP + 1):
                h, s = n // 6, n % 6
                q = n // UP - 1
                p = p_att + q
                tile = 2 * (q // 3)
                if n == 3:
                    chain.step(dve.memset(zz[:, :, 0:CONV_K - 1], 0.0))
                if n % UP == 0 and q % 3 == 1:
                    dve.wait_ge(unit_done, u_att + n)
                    dve.wait_ge(cc_ready, tile + 2)
                    for m in range(2):
                        chain.step(dve.tensor_tensor(zz[:, m, CONV_K - 1:], main[:, 2 * (p % 2) + m, :], cc[:, m],
                                                     ALU.mult))
                    chain.wait()
                    dve.sem_inc(set_free[p % 2], 1)
                if n % UP == 0 and n and q % 3 == 2:
                    dve.wait_ge(unit_done, u_att + n)
                    for m in range(2):
                        dve.tensor_tensor(cc[:, m], main[:, 2 * (p % 2) + m, :], cc[:, m], ALU.mult).then_inc(b_ready, 1)
                    dve.wait_ge(b_ready, tile + 2)
                    dve.sem_inc(set_free[p % 2], 1)
                    for m in range(2):
                        dve.wait_ge(b_hi, tile + m + 1)
                        dve.tensor_tensor(br_lo[:, 4 + tile + m, :], cc[:, m], br_hi[:, 4 + tile + m, :].bitcast(F32),
                                          ALU.subtract).then_inc(b_lo, 1)
                if s == 0 and n:
                    dve.wait_ge(c_hi, h)
                    dve.tensor_tensor(br_lo[:, 8 + h - 1, :], aux[:, 3, :], br_hi[:, 8 + h - 1, :].bitcast(F32),
                                      ALU.subtract).then_inc(c_lo, 1)
                if n == 6 * UP:
                    break
                if s == 0:
                    dve.wait_ge(bcast_done, 2 + h)
                    dve.scalar_tensor_tensor(kT[:, h, :], kT[:, h, :], gqk, aux[:, 0, :], ALU.mult,
                                             ALU.mult).then_inc(k_ready, 1)
                split_lo(dve, u_att + n + PREFETCH, n + PREFETCH)
                if n // UP % 3 == 2 and n % UP in (2, 4):
                    m = n % UP // 2 - 1
                    t = 2 * (n // UP // 3) + m
                    tap = [cst[:, C_CW + 4 * k + t:C_CW + 4 * k + t + 1] for k in range(CONV_K)]
                    chain.step(dve.tensor_scalar(cc[:, m], zz[:, m, 0:S], tap[0], None, ALU.mult))
                    for k in range(1, CONV_K):
                        chain.wait()
                        chain.step(dve.scalar_tensor_tensor(cc[:, m], zz[:, m, k:k + S], tap[k], cc[:, m],
                                                            ALU.mult, ALU.add))
                    chain.wait()
                if s == 2:
                    if h:
                        dve.wait_ge(turn_mm, h)
                    else:
                        dve.wait_ge(masks_ready, 1)
                    for n_t, i in enumerate((3, 2, 1, 0)):
                        bank, c0 = logit_at[i]
                        c = prob_at[i]
                        dve.wait_ge(logits_mm, 4 * h + n_t + 1)
                        chain.step(dve.tensor_tensor_reduce(
                            prob[:, c:c + P * (i + 1)], aux[:, bank, c0:c0 + P * (i + 1)], maskM[:, c:c + P * (i + 1)],
                            scale=rqk[:, 4 * h + i:4 * h + i + 1], scalar=EMPTY, op0=ALU.add, op1=ALU.max,
                            accum_out=mx[:, i:i + 1]))
                    chain.wait()
                    dve.tensor_scalar(nmx, mx, -1.0, None, ALU.mult).then_inc(max_ready, 1)
                if s == 3:
                    dve.wait_ge(exp_done, 4 * h + 4)
                    chain.step(dve.reciprocal(rinv, rsum))
                    chain.wait()
                    for i in range(TT):
                        c = prob_at[i]
                        ins = dve.tensor_scalar(prob[:, c:c + P * (i + 1)], prob[:, c:c + P * (i + 1)],
                                                rinv[:, i:i + 1], None, ALU.mult)
                    ins.then_inc(prob_ready, 1)
                    if h + 1 < ATTN_HEADS:
                        dve.wait_ge(bcast_done, 2 + h)
                        diagonals(dve, rqk, 32 + 4 * (h + 1), dg)
                if s == 4:
                    dve.wait_ge(turn_mm, h + 1)
                    if h:
                        dve.wait_ge(pv_mm, h)
                    dve.tensor_copy(probT[:, 2 * S:2 * S + 2 * P], aux[:, 2, 0:2 * P]).then_inc(turned_dve, 1)

            dve.wait_ge(b_lo, 4)
            dve.sem_inc(gate_used, 1)
            with dve.Fori(0, G_IT) as i:
                for j in range(G_U + 1):
                    if j in g_ends and g_ends.index(j) % 2 == 1:
                        q = g_ends.index(j)
                        b, parity = q // 2, (p_g + q) % 2
                        dve.wait_ge(unit_done, i * G_U + (u_g + j))
                        for m in range(2):
                            dve.wait_ge(sig_done, i * 6 + (2 * b + m + 1))
                            t = bass.ds(i * 2 + m, 1)
                            dst = gt[:, m:m + 1, :] if b else trunk[:, t, :]
                            dve.tensor_tensor(dst, main[:, 2 * parity + m:2 * parity + m + 1, :], sg[:, m:m + 1, :],
                                              ALU.mult).then_inc(gate_used, 1)
                        dve.wait_ge(gate_used, i * 6 + (2 * b + 3))
                        dve.sem_inc(set_free[parity], 1)
                        if b == 2:
                            dve.wait_ge(merged, i * 4 + 2)
                        for m in range(2 if b else 0):
                            t = bass.ds(i * 2 + m, 1)
                            dve.tensor_tensor(trunk[:, t, :], trunk[:, t, :], gt[:, m:m + 1, :],
                                              ALU.add).then_inc(merged, 1)
                    if j < G_U:
                        split_lo(dve, i * G_U + (u_g + j + PREFETCH), j + PREFETCH)

            for kt in range(KT):
                dve.wait_ge(m_hi, kt + 1)
                dve.tensor_tensor(act_lo[:, kt, :], trunk[:, kt, :], act_hi[:, kt, :].bitcast(F32),
                                  ALU.subtract).then_inc(m_ready, 1)

            with dve.Fori(0, 4) as i:
                for j in range(2 * UP):
                    split_lo(dve, i * (2 * UP) + (u_o + j + PREFETCH), j + PREFETCH)
                    if j % UP == UP - 1:
                        q = j // UP
                        parity = (p_o + q) % 2
                        dve.wait_ge(unit_done, i * (2 * UP) + (u_o + j + 1))
                        dve.wait_ge(xres_landed, i * 32 + 16 * (q + 1))
                        for m in range(2):
                            t = i * 4 + (2 * q + m)
                            dve.tensor_tensor(trunk[:, bass.ds(t, 1), :], main[:, 2 * parity + m:2 * parity + m + 1, :],
                                              xres[:, m:m + 1, :], ALU.add).then_inc(x2_ready, 1)
                        dve.wait_ge(x2_ready, i * 4 + (2 * q + 2))
                        dve.sem_inc(set_free[parity], 1)
                        for m in range(2):
                            t = i * 4 + (2 * q + m)
                            dve.wait_ge(x2_hi, t + 1)
                            dve.scalar_tensor_tensor(br_lo[:, bass.ds(t, 1), :], trunk[:, bass.ds(t, 1), :],
                                                     cst[:, bass.ds(t + C_G2, 1)],
                                                     br_hi[:, bass.ds(t, 1), :].bitcast(F32),
                                                     ALU.mult, ALU.subtract).then_inc(x2_lo, 1)

            scale_of_tokens(18, 3, r4, ms4, nt4, aux[:, 3, 0:TT], D)
            diagonals(dve, r4, 0, ft[:, 1])
            dve.wait_ge(r2_ready, 1)

            def hidden_chunk(c, last):
                with dve.Fori(0, 4) as i:
                    for j in range(2 * UP):
                        split_lo(dve, c * CH_U + i * (2 * UP) + (u_f + j + PREFETCH), j + PREFETCH)
                        if j % UP == UP - 1:
                            q = j // UP
                            parity = (p_f + q) % 2
                            dve.wait_ge(unit_done, c * CH_U + i * (2 * UP) + (u_f + j + 1))
                            for m in range(2):
                                dve.tensor_tensor(ft[:, m], main[:, 2 * parity + m, :], r2B[:, :],
                                                  ALU.mult).then_inc(f_scaled, 1)
                            dve.wait_ge(f_scaled, c * KT + i * 4 + (2 * q + 2))
                            dve.sem_inc(set_free[parity], 1)
                            for m in range(2):
                                dve.scalar_tensor_tensor(ff[:, m], ft[:, m], 0.0, ft[:, m], ALU.max,
                                                         ALU.mult).then_inc(f_ready, 1)
                            for m in range(2):
                                t = i * 4 + (2 * q + m)
                                dve.wait_ge(f_hi, c * KT + t + 1)
                                dve.tensor_tensor(act_lo[:, bass.ds(t, 1), :], ff[:, m:m + 1, :],
                                                  act_hi[:, bass.ds(t, 1), :].bitcast(F32),
                                                  ALU.subtract).then_inc(f_lo, 1)

                def y_pass(i, q, n_splits):
                    for j in range(n_splits):
                        split_lo(dve, c * CH_U + i * (2 * UP) + (u_f + (8 + q) * UP + j + PREFETCH), j + PREFETCH)
                    parity = (p_f + q) % 2
                    dve.wait_ge(unit_done, c * CH_U + i * (2 * UP) + (u_f + (9 + q) * UP))
                    for m in range(2):
                        t = bass.ds(i * 4 + (2 * q + m), 1)
                        dve.tensor_tensor(trunk[:, t, :], main[:, 2 * parity + m:2 * parity + m + 1, :], trunk[:, t, :],
                                          ALU.add).then_inc(y_ready, 1)
                    dve.wait_ge(y_ready, c * KT + i * 4 + (2 * q + 2))
                    dve.sem_inc(set_free[parity], 1)

                with dve.Fori(0, 3) as i:
                    y_pass(i, 0, UP)
                    y_pass(i, 1, UP)
                y_pass(3, 0, UP)
                y_pass(3, 1, UP - PREFETCH if last else UP)

            with dve.Fori(0, CH - 1) as c:
                hidden_chunk(c, False)
            hidden_chunk(CH - 1, True)

        @block.gpsimd
        def _(pool):
            pool.wait_ge(k_ready, ATTN_HEADS)
            pool.memset(ssq[:, :], 0.0).then_inc(x2_added, 1)
            with pool.Fori(0, KT) as t:
                pool.wait_ge(x2_squared, t + 1)
                pool.wait_ge(x2_added, t + 1)
                pool.tensor_tensor(ssq[:, :], ssq[:, :], sq[:, 0], ALU.add).then_inc(x2_added, 1)
            for n in range(8):
                pool.wait_ge(y_ready, (CH - 1) * KT + 2 * n + 2)
                pool.dma_start(outT[n * COLS:(n + 1) * COLS, :].rearrange("(m p) s -> p m s", p=P),
                               trunk[:, 2 * n:2 * n + 2, :]).then_inc(out_written, 16)
            pool.wait_ge(out_written, 8 * 16)


def constants(norm1, norm2, pool_scale, conv_w, q_gain, k_gain):
    import numpy as np

    def by_tile(a):
        return np.ascontiguousarray(a).reshape(-1, P).T

    inv = np.array([[1.0 / min(t + 1, w) for w in POOL_WINDOWS for t in range(16)]], np.float32)
    parts = [by_tile(norm1), by_tile(norm2), by_tile(pool_scale), by_tile(conv_w), by_tile(q_gain),
             by_tile(k_gain), np.repeat(inv, P, axis=0), np.eye(P, dtype=np.float32), np.ones((P, P), np.float32)]
    return np.concatenate([np.asarray(a, np.float32) for a in parts], axis=1)


def kernel(**inputs):
    import numpy as np
    import concourse.bacc as bacc
    from concourse.bass_utils import run_bass_kernel_spmd

    a = {k: np.asarray(v) for k, v in inputs.items()}
    x = a["x"]
    arrays = {
        "xT": np.ascontiguousarray(x[0].T),
        "cst": constants(a["norm1"][0], a["norm2"][0], a["pool_scale"][0], a["conv_w"][0], a["q_gain"][0], a["k_gain"][0]),
    }
    for name in ("w_in", "pool_w", "w_pool_out", "w_conv_out", "w_attn_out", "w_o", "w_ff1", "w_ff2"):
        arrays[name] = np.ascontiguousarray(a[name][0])
    nc = bacc.Bacc("TRN2", target_bir_lowering=False, num_devices=1)
    args = [nc.dram_tensor(n, v.shape, mybir.dt.from_np(v.dtype), kind="ExternalInput").ap() for n, v in arrays.items()]
    args.append(nc.dram_tensor("outT", arrays["xT"].shape, F32, kind="ExternalOutput").ap())
    build(nc, *args)
    r = run_bass_kernel_spmd(nc, [arrays], core_ids=[0])
    return np.ascontiguousarray(r.results[0]["outT"].T)[None]
```

```python
from contextlib import ExitStack

import concourse.bass as bass
from concourse import mybir

F32 = mybir.dt.float32
F32R = mybir.dt.float32r
ALU = mybir.AluOpType
ACT = mybir.ActivationFunctionType

P = 128
COLS = 256
UK = 2
SLOTS = 4
RAWS = 4
PREFETCH = 3
XG_AHEAD = 2
SUMS_AT = 8
SPREAD_AT = 9
EPS = 1e-6
MASKED = -1e36
EMPTY = -3.0e38

POOL_WINDOWS = (2, 4, 8, 16)
CONV_K = 3
CHUNK = 64
TOPK_MAX = 256
IDX_HEADS = 8
IDX_DIM = 64
ATTN_HEADS = 8

C_G1, C_G2, C_PS, C_CW, C_QG, C_KG, C_INV = 0, 16, 32, 36, 48, 49, 50
C_ID = C_INV + len(POOL_WINDOWS) * 16
C_ONE = C_ID + P
C_N = C_ONE + P


def build(nc, xT, cst_dram, w_in, pool_w, w_po, w_co, w_ao, w_o, w_f1, w_f2, outT):
    D, S = xT.shape
    FF = w_f1.shape[1]
    KT = D // P
    TT = S // P
    TOPK = min(TOPK_MAX, S // 4)
    HD = D // 16
    PW = D // 4
    AW = ATTN_HEADS * HD
    NW = len(POOL_WINDOWS)
    assert S == 512 and TOPK == P and HD == P and KT == 16 and TT == 4

    c_pool, c_b, c_c, c_x = 0, PW, 2 * PW, 3 * PW
    c_q = 4 * PW
    c_v, c_qi = c_q + 2 * AW, c_q + 3 * AW
    c_ki = c_qi + IDX_HEADS * IDX_DIM
    c_gate = c_ki + IDX_DIM + IDX_HEADS
    KIW = IDX_DIM + IDX_HEADS

    UP = KT // UK
    u_idx = 0
    u_qk, p_qk = 5 * UP, 5
    u_v, p_v = u_qk + 8 * UP, p_qk + 8
    u_att, p_att = u_v + 4 * UP, p_v + 4
    u_g, p_g = u_att + 6 * UP, p_att + 6
    G_U, G_P, G_IT = 4 * UP, 6, D // COLS
    u_o, p_o = u_g + G_IT * G_U, p_g + G_IT * G_P
    u_f, p_f = u_o + 8 * UP, p_o + 8
    CH = FF // D
    CH_U, CH_P = 16 * UP, 16
    g_ends = (8, 10, 18, 20, 28, 32)

    ctx = ExitStack()
    with ctx:
        base = -(-nc.sbuf_base // 32) * 32

        def at(name, shape, dt, offset):
            return nc.alloc_sbuf_tensor_at(name, shape, dt, offset=base + offset)

        KB = 1024
        act_hi = at("act_hi", [P, KT, S], F32R, 0)
        act_lo = at("act_lo", [P, KT, S], F32R, 32 * KB)
        BR = 64 * KB
        br_hi = at("br_hi", [P, KT, S], F32R, BR)
        br_lo = at("br_lo", [P, KT, S], F32R, BR + 32 * KB)
        qT = at("qT", [P, ATTN_HEADS, S], F32, BR + 16 * KB)
        kT = at("kT", [P, ATTN_HEADS, S], F32, BR + 48 * KB)
        poolT = at("poolT", [P, NW, S], F32, BR + 32 * KB)
        QI_TILE = 4
        qiT = at("qiT", [P, 4, S], F32, BR + QI_TILE * 2 * KB)
        kiT = at("kiT", [P, S], F32, BR + 40 * KB)
        score = [at(f"score{i}", [P, P * (i + 1)], F32, BR + (42 * 1024 + o)) for i, o in ((1, 0), (2, 1024), (3, 2560))]
        M = 128 * KB
        xin = at("xin", [P, KT, S], F32, M)
        vv = at("v", [P, TT, AW], F32, M)
        work = [at(f"work{i}", [P, P * (i + 1)], F32, M + o) for i, o in ((1, 0), (2, 1024), (3, 2560))]
        PCOLS = P * (1 + 2 + 3 + 4)
        maskM = at("maskM", [P, PCOLS], F32, M + 16 * KB)
        prob = at("prob", [P, PCOLS], F32, M + 21 * KB)
        probT = at("probT", [P, PCOLS], F32, M + 26 * KB)
        trunk = at("trunk", [P, KT, S], F32, M)
        R = 160 * KB
        w_hi = at("w_hi", [P, SLOTS, UK, COLS], F32R, R)
        w_lo = at("w_lo", [P, SLOTS, UK, COLS], F32R, R + 8 * KB)
        w_raw = at("w_raw", [P, RAWS, 2 * UK, COLS], F32, R + 16 * KB)
        T = 192 * KB
        cst = at("cst", [P, C_N], F32, T)
        poolw = at("poolw", [P, NW, P], F32, T + 1504)
        st = at("st", [P, 512], F32, T + 3552)
        T = T + 5600
        sq = at("sq", [P, 2, S], F32, T)
        rB = at("rB", [P, S], F32, T)
        wiT = at("wiT", [P, S], F32, T)
        PADW = 16
        U = at("U", [P, 2, PADW + S], F32, T)
        Sa = at("Sa", [P, 2, PADW + S], F32, T + 4224)
        zz = at("zz", [P, 2, CONV_K - 1 + S], F32, T)
        cc = at("cc", [P, 2, S], F32, T + 4128)
        sg = at("sg", [P, 2, S], F32, T)
        gt = at("gt", [P, 2, S], F32, T + 4096)
        xres = at("xres", [P, 2, S], F32, T + 4096)
        dg = at("dg", [P, S], F32, T + 8224)
        r2B = at("r2B", [P, S], F32, T)
        ft = at("ft", [P, 2, S], F32, T + 2048)
        ff = at("ff", [P, 2, S], F32, T + 6144)
        ssq = at("ssq", [P, S], F32, T + 8224)

        ident = cst[:, C_ID:C_ID + P]
        ones = cst[:, C_ONE:C_ONE + P]

        rqk = st[:, 0:64]
        ms64, nt64 = st[:, 64:128], st[:, 128:192]
        gqk = st[:, 192:193]
        ws = st[:, 200:200 + TT * IDX_HEADS]
        top8 = [st[:, 240 + 8 * i:248 + 8 * i] for i in range(3)]
        need = st[:, 270:273]
        rsum, nmx, rinv = st[:, 280:284], st[:, 284:288], st[:, 288:292]
        r4, ms4, nt4 = st[:, 300:304], st[:, 304:308], st[:, 308:312]

        main = ctx.enter_context(nc.psum_tensor("main", [P, 4, S], F32))
        aux = ctx.enter_context(nc.psum_tensor("aux", [P, 4, S], F32))

        def sem(name):
            return ctx.enter_context(nc.semaphore(name))

        raw_landed = [sem(f"raw_landed{i}") for i in range(RAWS)]
        hi_ready, lo_ready, unit_done = sem("hi_ready"), sem("lo_ready"), sem("unit_done")
        set_free = [sem("set_free0"), sem("set_free1")]
        x_landed = [sem(f"x_landed{i}") for i in range(8)]
        cst_landed, poolw_landed, ki_doubled = sem("cst_landed"), sem("poolw_landed"), sem("ki_doubled")
        x_squared, x_summed = sem("x_squared"), sem("x_summed")
        sums_done, root_done = sem("sums_done"), sem("root_done")
        diag_ready, bcast_done = sem("diag_ready"), sem("bcast_done")
        ms_ready = sem("ms_ready")
        h_hi, h_lo_even, h_lo_odd = sem("h_hi"), sem("h_lo_even"), sem("h_lo_odd")
        st_cleared = sem("st_cleared")
        xg_hi, xg_lo, h_scaled, r1_ready = sem("xg_hi"), sem("xg_lo"), sem("h_scaled"), sem("r1_ready")
        ki_ready, qi_ready, wi_turned, ws_ready = sem("ki_ready"), sem("qi_ready"), sem("wi_turned"), sem("ws_ready")
        score_mm, relu_done, score_added = sem("score_mm"), sem("relu_done"), sem("score_added")
        pool_u, pool_diff, pool_mm, a_hi, a_lo = sem("pool_u"), sem("pool_diff"), sem("pool_mm"), sem("a_hi"), sem("a_lo")
        qk_ready, qk_squared, v_ready = sem("qk_ready"), sem("qk_squared"), sem("v_ready")
        k_ready = sem("k_ready")
        masks_ready = sem("masks_ready")
        logits_mm, max_ready, exp_done, prob_ready = sem("logits_mm"), sem("max_ready"), sem("exp_done"), sem("prob_ready")
        turn_mm, turned_act, turned_dve, pv_mm, c_hi, c_lo = (
            sem("turn_mm"), sem("turned_act"), sem("turned_dve"), sem("pv_mm"), sem("c_hi"), sem("c_lo"))
        cc_ready, b_ready, b_hi, b_lo = sem("cc_ready"), sem("b_ready"), sem("b_hi"), sem("b_lo")
        sig_done, gate_used = sem("sig_done"), sem("gate_used")
        m_ready, m_hi = sem("m_ready"), sem("m_hi")
        xres_landed = sem("xres_landed")
        x2_ready, x2_hi, x2_squared, x2_added, x2_lo = (
            sem("x2_ready"), sem("x2_hi"), sem("x2_squared"), sem("x2_added"), sem("x2_lo"))
        r2_ready = sem("r2_ready")
        f_ready, f_hi, f_lo = sem("f_ready"), sem("f_hi"), sem("f_lo")
        y_ready, out_written, last_written = sem("y_ready"), sem("out_written"), sem("last_written")
        dve_chain, pads_ready, merged = sem("dve_chain"), sem("pads_ready"), sem("merged")
        topk_done, f_scaled = sem("topk_done"), sem("f_scaled")

        class Chain:

            def __init__(self, eng, s):
                self.eng, self.sem, self.n = eng, s, 0

            def step(self, ins):
                ins.then_inc(self.sem, 1)
                self.n += 1

            def wait(self):
                self.eng.wait_ge(self.sem, self.n)

        def wait_apart(eng, s, value):
            value = eng.snap(value)
            eng.wait_ge(cst_landed, 16)
            eng.wait_ge(s, value)

        logit_at = {3: (0, 0), 2: (1, 0), 0: (1, 3 * P), 1: (2, 0)}
        prob_at = {i: P * i * (i + 1) // 2 for i in range(TT)}
        turn_at = {0: (0, 0), 1: (1, 0), 2: (2, 0), 3: (1, 3 * P)}
        probT_at = {0: 0, 1: 4 * P, 3: 7 * P, 2: 8 * P}


        def split_hi(act, g, j, width=COLS):
            act.wait_ge(raw_landed[(j // 2) % RAWS], raw_count(g, j))
            if not isinstance(g, int) or g >= SLOTS:
                act.wait_ge(unit_done, g - SLOTS + 1)
            act.activation(w_hi[:, j % SLOTS, :, 0:width],
                           w_raw[:, (j // 2) % RAWS, UK * (j % 2):UK * (j % 2) + UK, 0:width],
                           ACT.Copy).then_inc(hi_ready, 1)

        def split_lo(dve, g, j, width=COLS):
            dve.wait_ge(hi_ready, g + 1)
            dve.tensor_tensor(w_lo[:, j % SLOTS, :, 0:width],
                              w_raw[:, (j // 2) % RAWS, UK * (j % 2):UK * (j % 2) + UK, 0:width],
                              w_hi[:, j % SLOTS, :, 0:width].bitcast(F32), ALU.subtract).then_inc(lo_ready, 1)

        def raw_count(g, j):
            if isinstance(g, int):
                return 16 * (g // 8 + 1)
            return (g - j % 8) * 2 + 16

        def split_any(split, eng, g, j):
            split(eng, g, j, KIW if 2 * UP <= g < 3 * UP else COLS)

        def unit(pe, g, j, kt0, last_kt, bank, hi, lo, width=COLS):
            pe.wait_ge(lo_ready, g + 1)
            for k in range(UK):
                kt = kt0 + k
                for m in range(-(-width // P)):
                    c0, c1 = m * P, min(width, m * P + P)
                    out = main[0:c1 - c0, bank + m, :]
                    wh, wl = w_hi[:, j % SLOTS, k, c0:c1], w_lo[:, j % SLOTS, k, c0:c1]
                    pe.matmul(out, wh, hi[:, kt, :], start=(kt == last_kt[0]), stop=False)
                    pe.matmul(out, wh, lo[:, kt, :], start=False, stop=False)
                    mm = pe.matmul(out, wl, hi[:, kt, :], start=False, stop=(kt == last_kt[1]))
            mm.then_inc(unit_done, 1)

        def wait_set(pe, p, parity, n=None):
            if n is None:
                n = p // 2
            if not isinstance(n, int) or n >= 1:
                pe.wait_ge(set_free[parity], n)

        def token_sums(pe, square, column0, bank):
            for t in range(TT):
                mm = pe.matmul(aux[:, bank, column0 + t:column0 + t + 1], square[:, t * P:(t + 1) * P],
                               ones[:, 0:1], start=True, stop=True)
            return mm

        def newton(dve, chain, r, ms, tmp, out):
            chain.step(dve.tensor_tensor(tmp, r, r, ALU.mult))
            chain.wait()
            chain.step(dve.tensor_tensor(tmp, tmp, ms, ALU.mult))
            chain.wait()
            chain.step(dve.tensor_scalar(tmp, tmp, -0.5, 1.5, ALU.mult, ALU.add))
            chain.wait()
            return dve.tensor_tensor(out, r, tmp, ALU.mult)

        def diagonals(dve, r, column0, dg):
            for t in range(TT):
                ins = dve.tensor_scalar(dg[:, t * P:(t + 1) * P], ident, r[:, column0 + t:column0 + t + 1],
                                        None, ALU.mult)
            ins.then_inc(diag_ready, 1)

        block = ctx.enter_context(nc.Block())

        @block.sync
        def _(sp):
            def load(L, slot, w, row0, col0, width=COLS):
                if not isinstance(L, int) or L >= RAWS:
                    sp.wait_ge(lo_ready, (L - RAWS) * 2 + 2)
                rows = w[bass.ds(row0, 2 * UK * P), bass.ds(col0, width)].rearrange("(t p) c -> p t c", p=P)
                sp.dma_start(w_raw[:, slot, :, 0:width], rows).then_inc(raw_landed[slot], 16)

            LP = UP // 2
            def load_x(i):
                sp.dma_start(xin[:, 2 * i:2 * i + 2, :],
                             xT[2 * i * P:(2 * i + 2) * P, :].rearrange("(t p) s -> p t s", p=P)
                             ).then_inc(x_landed[i], 16)

            sp.dma_start(cst[:], cst_dram).then_inc(cst_landed, 16)
            for n in range(LP):
                load_x(2 * n)
                load(n, n % RAWS, w_in, n * 2 * UK * P, c_qi)
                load_x(2 * n + 1)
            for i, (col, width) in enumerate(((c_qi, COLS), (c_qi + COLS, COLS), (c_ki, KIW),
                                              (c_pool, COLS), (c_pool + COLS, COLS))):
                if i == 1:
                    sp.dma_start(poolw[:], pool_w.rearrange("g c d -> c g d")).then_inc(poolw_landed, 16)
                for n in range(LP if i else 0):
                    load(i * LP + n, n % RAWS, w_in, n * 2 * UK * P, col, width)
            with sp.Fori(0, 8) as i:
                for n in range(LP):
                    load(i * LP + (u_qk // 2 + n), n % RAWS, w_in, n * 2 * UK * P, i * COLS + c_q)
            with sp.Fori(0, 4) as i:
                for n in range(LP):
                    load(i * LP + (u_v // 2 + n), n % RAWS, w_in, n * 2 * UK * P, i * COLS + c_v)
            for i, col in enumerate((c_c, c_x, c_b, c_c + COLS, c_x + COLS, c_b + COLS)):
                for n in range(LP):
                    load(u_att // 2 + i * LP + n, n % RAWS, w_in, n * 2 * UK * P, col)
            with sp.Fori(1, G_IT + 1) as next_i:
                i = next_i - 1
                n_load = 0
                for b, (w, loads) in enumerate(((w_po, 1), (w_co, 1), (w_ao, 2))):
                    for n in range(LP):
                        load(i * (G_U // 2) + (u_g // 2 + n_load), n_load % RAWS, w_in, n * 2 * UK * P,
                             i * COLS + (c_gate + b * D))
                        n_load += 1
                    for n in range(loads):
                        load(i * (G_U // 2) + (u_g // 2 + n_load), n_load % RAWS, w, n * 2 * UK * P,
                             next_i * COLS - COLS)
                        n_load += 1
            with sp.Fori(0, 8) as i:
                for n in range(LP):
                    load(i * LP + (u_o // 2 + n), n % RAWS, w_o, n * 2 * UK * P, i * COLS)
            with sp.Fori(0, CH) as c:
                with sp.Fori(0, 8) as i:
                    for n in range(LP):
                        load(c * (CH_U // 2) + i * LP + (u_f // 2 + n), n % RAWS, w_f1, n * 2 * UK * P,
                             c * D + i * COLS)
                with sp.Fori(0, 8) as i:
                    for n in range(LP):
                        load(c * (CH_U // 2) + i * LP + (u_f // 2 + CH_U // 4 + n), n % RAWS, w_f2,
                             c * D + n * 2 * UK * P, i * COLS)
            for t in (KT - 2, KT - 1):
                sp.wait_ge(y_ready, (CH - 1) * KT + t + 1)
                sp.dma_start(outT[t * P:(t + 1) * P, :], trunk[:, t, :]).then_inc(last_written, 16)
            sp.wait_ge(last_written, 2 * 16)

        @block.tensor
        def _(pe):
            H = (0, KT - 1)
            def score_product(n):
                i, h = 1 + n // 8, n % 8
                if n == 0:
                    pe.wait_ge(ki_doubled, 16)
                    pe.wait_ge(qi_ready, 4)
                if n >= 2:
                    pe.wait_ge(relu_done, n - 1)
                lo_p = IDX_DIM * (h % 2)
                pe.matmul(aux[:, n % 2, 0:P * (i + 1)], qiT[lo_p:lo_p + IDX_DIM, h // 2, i * P:(i + 1) * P],
                          kiT[lo_p:lo_p + IDX_DIM, 0:P * (i + 1)], start=True, stop=True).then_inc(score_mm, 1)

            for p in range(5):
                wait_set(pe, p, p % 2)
                for j in range(UP):
                    g = p * UP + j
                    if p == 0:
                        pe.wait_ge(xg_lo, 2 * j + 2)
                    if p == 2:
                        pe.wait_ge(h_lo_even, j + 1)
                        pe.wait_ge(h_lo_odd, j + 1)
                    if g == SUMS_AT:
                        pe.wait_ge(cst_landed, 16)
                        pe.wait_ge(x_summed, KT)
                        token_sums(pe, dg, 0, 3).then_inc(sums_done, 1)
                    if g == SPREAD_AT:
                        pe.wait_ge(diag_ready, 1)
                        pe.matmul(aux[:, 0, :], ones, dg[:, :], start=True, stop=True).then_inc(bcast_done, 1)
                    if p == 3 and j == 2:
                        pe.wait_ge(ki_ready, 2)
                        for t in range(TT):
                            mm = pe.transpose(aux[:, 3, 16 + 8 * t:24 + 8 * t], wiT[IDX_DIM:KIW, t * P:(t + 1) * P],
                                              cst[IDX_DIM:KIW, C_ID + IDX_DIM:C_ID + KIW])
                        mm.then_inc(wi_turned, 1)
                    s = (p - 3) * UP + j - 3
                    if p >= 3 and 0 <= s < 12:
                        score_product(2 * s)
                        score_product(2 * s + 1)
                    hi, lo = (br_hi, br_lo) if p < 2 else (act_hi, act_lo)
                    unit(pe, g, j, 2 * j, H, 2 * (p % 2), hi, lo, KIW if p == 2 else COLS)

            def pass_pair(u0, hi, lo, p0, n0, n1):
                for q in range(2):
                    parity = (p0 + q) % 2
                    wait_set(pe, None, parity, (n0, n1)[q])
                    for j in range(UP):
                        unit(pe, u0 + (q * UP + j), j, 2 * j, H, 2 * parity, hi, lo)

            with pe.Fori(0, 4) as i:
                pass_pair(i * (2 * UP) + u_qk, act_hi, act_lo, p_qk, i + p_qk // 2, i + (p_qk + 1) // 2)

            def k_spread(h):
                pe.wait_ge(diag_ready, 2 + h)
                if h >= 1:
                    pe.wait_ge(turned_act, 2 * h)
                else:
                    pe.wait_ge(a_lo, NW)
                pe.matmul(aux[:, 0, :], ones, dg[:, :], start=True, stop=True).then_inc(bcast_done, 1)

            for q in range(4):
                p = p_v + q
                wait_set(pe, p, p % 2)
                for j in range(UP):
                    g = u_v + q * UP + j
                    n = q * UP + j
                    if 1 <= n <= 16:
                        pe.wait_ge(qk_squared, n)
                        if n == 1:
                            pe.wait_ge(ws_ready, 1)
                        token_sums(pe, sq[:, (n - 1) % 2], 4 * (n - 1), 3).then_inc(sums_done, 1)
                    if 16 <= n < 16 + NW:
                        gr = n - 16
                        if gr == 0:
                            pe.wait_ge(relu_done, 24)
                            pe.wait_ge(poolw_landed, 16)
                            pe.wait_ge(pool_diff, NW)
                        if gr >= 2:
                            pe.wait_ge(a_lo, gr - 1)
                        pe.matmul(aux[:, gr % 2, :], poolw[:, gr, :], poolT[:, gr, :], start=True,
                                  stop=True).then_inc(pool_mm, 1)
                    if n == 4 * UP - 1:
                        k_spread(0)
                    pe.wait_ge(lo_ready, g + 1)
                    for k in range(UK):
                        kt = 2 * j + k
                        for t in range(TT):
                            out = main[:, 2 * (p % 2) + t // 2, (t % 2) * COLS:(t % 2 + 1) * COLS]
                            th, tl = act_hi[:, kt, t * P:(t + 1) * P], act_lo[:, kt, t * P:(t + 1) * P]
                            wh, wl = w_hi[:, j % SLOTS, k, :], w_lo[:, j % SLOTS, k, :]
                            pe.matmul(out, th, wh, start=(kt == 0 and t % 2 == 0), stop=False, skip_group_check=True)
                            pe.matmul(out, th, wl, start=False, stop=False, skip_group_check=True)
                            mm = pe.matmul(out, tl, wh, start=False, stop=(kt == KT - 1), skip_group_check=True)
                    mm.then_inc(unit_done, 1)


            def logits(h):
                pe.wait_ge(k_ready, h + 1)
                if h >= 1:
                    pe.wait_ge(turned_act, 2 * h)
                    pe.wait_ge(turned_dve, h)
                for i in (3, 0, 2, 1):
                    bank, c0 = logit_at[i]
                    pe.matmul(aux[:, bank, c0:c0 + P * (i + 1)], qT[:, h, i * P:(i + 1) * P],
                              kT[:, h, 0:P * (i + 1)], start=True, stop=True).then_inc(logits_mm, 1)

            def turns(h):
                pe.wait_ge(prob_ready, h + 1)
                for kb in range(TT):
                    bank, c0 = turn_at[kb]
                    for i in range(kb, TT):
                        c = prob_at[i] + kb * P
                        mm = pe.transpose(aux[:, bank, c0 + (i - kb) * P:c0 + (i - kb + 1) * P],
                                          prob[:, c:c + P], ident)
                mm.then_inc(turn_mm, 1)

            def pv(h):
                pe.wait_ge(turned_act, 2 * h + 2)
                pe.wait_ge(turned_dve, h + 1)
                if h == 0:
                    pe.wait_ge(v_ready, 8)
                else:
                    pe.wait_ge(c_lo, h)
                for kb in range(TT):
                    n = (TT - kb) * P
                    mm = pe.matmul(aux[:, 3, kb * P:S], vv[:, kb, h * HD:(h + 1) * HD],
                                   probT[:, probT_at[kb]:probT_at[kb] + n], start=(kb == 0), stop=(kb == TT - 1),
                                   skip_group_check=True)
                mm.then_inc(pv_mm, 1)

            for q in range(6):
                p = p_att + q
                wait_set(pe, p, p % 2)
                for j in range(UP):
                    n = q * UP + j
                    h, s = n // 6, n % 6
                    if s == 1:
                        logits(h)
                    elif s == 4:
                        turns(h)
                    elif s == 5:
                        pv(h)
                        if h + 1 < ATTN_HEADS:
                            k_spread(h + 1)
                    unit(pe, u_att + n, j, 2 * j, H, 2 * (p % 2), act_hi, act_lo)

            with pe.Fori(0, G_IT) as i:
                j = 0
                for b, (t0, units) in enumerate(((0, 2), (4, 2), (8, 4))):
                    for gate in (True, False):
                        q = 2 * b + (not gate)
                        p = p_g + q
                        wait_set(pe, None, p % 2, i * (G_P // 2) + p // 2)
                        if not gate:
                            if b == 0:
                                pe.wait_ge(a_lo, NW)
                            elif b == 1:
                                pe.wait_ge(b_lo, 4)
                            else:
                                pe.wait_ge(c_lo, ATTN_HEADS)
                        for n in range(UP if gate else units):
                            g = i * G_U + (u_g + j)
                            if gate:
                                unit(pe, g, j, 2 * n, H, 2 * (p % 2), act_hi, act_lo)
                            else:
                                unit(pe, g, j, t0 + 2 * n, (t0, t0 + 2 * units - 1), 2 * (p % 2), br_hi, br_lo)
                            j += 1

            with pe.Fori(0, 4) as i:
                for q in range(2):
                    p = p_o + q
                    wait_set(pe, None, p % 2, i + p // 2)
                    for j in range(UP):
                        if q == 0:
                            pe.wait_ge(m_ready, 2 * j + 2)
                        unit(pe, i * (2 * UP) + (u_o + q * UP + j), j, 2 * j, H, 2 * (p % 2), act_hi, act_lo)

            def hidden_chunk(c, first=False):
                free0, free1 = c * (CH_P // 2) + p_f // 2, c * (CH_P // 2) + (p_f + 1) // 2
                if first:
                    for q in range(2):
                        wait_set(pe, p_f + q, (p_f + q) % 2)
                        for j in range(UP):
                            if q == 0:
                                pe.wait_ge(x2_lo, 2 * j + 2)
                            if q == 0 and j == 3:
                                pe.wait_ge(x2_added, KT + 1)
                                token_sums(pe, ssq, 0, 3).then_inc(sums_done, 1)
                            if q == 0 and j == 5:
                                pe.wait_ge(diag_ready, 2 + ATTN_HEADS)
                                pe.matmul(aux[:, 0, :], ones, ft[:, 1, :], start=True,
                                          stop=True).then_inc(bcast_done, 1)
                            unit(pe, u_f + q * UP + j, j, 2 * j, H, 2 * ((p_f + q) % 2), br_hi, br_lo)
                with pe.Fori(1 if first else 0, 4) as i:
                    pass_pair(c * CH_U + i * (2 * UP) + u_f, br_hi, br_lo, p_f, i + free0, i + free1)
                with pe.Fori(0, 4) as i:
                    for q in range(2):
                        p = p_f + q
                        wait_set(pe, None, p % 2, c * (CH_P // 2) + i + (4 + p // 2))
                        for j in range(UP):
                            if q == 0:
                                pe.wait_ge(f_lo, c * KT + (2 * j + 2))
                            unit(pe, c * CH_U + i * (2 * UP) + (u_f + 8 * UP + q * UP + j), j, 2 * j, H,
                                 2 * (p % 2), act_hi, act_lo)

            hidden_chunk(0, first=True)
            with pe.Fori(1, CH) as c:
                hidden_chunk(c)

        @block.scalar
        def _(act):
            act.wait_ge(st_cleared, 1)
            act.activation(st[:, 511:512], st[:, 510:511], ACT.Copy)

            def xg_tile(kt):
                if kt == 0:
                    act.wait_ge(cst_landed, 16)
                if kt % 2 == 0:
                    act.wait_ge(x_landed[kt // 2], 16)
                act.activation(br_hi[:, kt, :], xin[:, kt, :], ACT.Copy,
                               scale=cst[:, C_G1 + kt:C_G1 + kt + 1]).then_inc(xg_hi, 1)

            def square(kt):
                if kt >= 2:
                    act.wait_ge(x_summed, kt - 1)
                act.activation(sq[:, kt % 2], xin[:, kt, :], ACT.Square).then_inc(x_squared, 1)

            for kt in range(2 * XG_AHEAD):
                xg_tile(kt)
                if kt % 2:
                    split_any(split_hi, act, kt // 2, kt // 2)
                    square(kt - 1)
                    square(kt)
            for g in range(XG_AHEAD, PREFETCH):
                split_any(split_hi, act, g, g)

            def h_tile(kt):
                act.wait_ge(h_scaled, kt + 1)
                act.activation(act_hi[:, kt, :], xin[:, kt, :], ACT.Copy).then_inc(h_hi, 1)

            def v_evict(act, q):
                p = p_v + q
                act.wait_ge(unit_done, u_v + (q + 1) * UP)
                if q == 0:
                    act.wait_ge(topk_done, 1)
                for b in range(2):
                    act.activation(vv[:, 2 * b:2 * b + 2, q * COLS:(q + 1) * COLS],
                                   main[:, 2 * (p % 2) + b, :].rearrange("p (t c) -> p t c", t=2),
                                   ACT.Copy).then_inc(v_ready, 1)
                act.wait_ge(v_ready, 2 * q + 2)
                act.sem_inc(set_free[p % 2], 1)

            def relu_scores(n):
                i = 1 + n // 8
                act.wait_ge(score_mm, n + 1)
                if n >= 2:
                    act.wait_ge(score_added, n - 1)
                act.activation(prob[:, (n % 2) * S:(n % 2) * S + P * (i + 1)], aux[:, n % 2, 0:P * (i + 1)],
                               ACT.Relu).then_inc(relu_done, 1)

            def pool_copy(m, bank):
                if m >= 2:
                    act.wait_ge(pool_diff, m - 1)
                act.activation(U[:, m % 2, PADW:], bank, ACT.Copy).then_inc(pool_u, 1)

            for g in range(u_idx, u_qk):
                if g < UP:
                    for kt in range(2 * (g + XG_AHEAD), min(2 * (g + XG_AHEAD) + 2, KT)):
                        xg_tile(kt)
                        square(kt)
                if g == SUMS_AT:
                    act.wait_ge(ms_ready, 1)
                    act.activation(r4, ms4, ACT.Sqrt).then_inc(root_done, 1)
                if g == SPREAD_AT:
                    act.wait_ge(bcast_done, 1)
                    act.activation(rB[:, :], aux[:, 0, :], ACT.Copy).then_inc(r1_ready, 1)
                if 0 <= g - SPREAD_AT < UP:
                    h_tile(2 * (g - SPREAD_AT))
                    h_tile(2 * (g - SPREAD_AT) + 1)
                if g == 3 * UP:
                    act.wait_ge(unit_done, g)
                    act.activation(kiT[0:IDX_DIM, :], main[0:IDX_DIM, 0, :], ACT.Copy).then_inc(ki_ready, 1)
                    act.activation(wiT[IDX_DIM:KIW, :], main[IDX_DIM:KIW, 0, :], ACT.Copy).then_inc(ki_ready, 1)
                    act.wait_ge(ki_ready, 2)
                    act.dma_start(kiT[IDX_DIM:2 * IDX_DIM, :], kiT[0:IDX_DIM, :]).then_inc(ki_doubled, 16)
                    act.sem_inc(set_free[0], 1)
                if g == 4 * UP:
                    act.wait_ge(unit_done, g)
                    act.wait_ge(pads_ready, 1)
                    for m in range(2):
                        pool_copy(m, main[:, 2 + m, :])
                    act.wait_ge(pool_u, 2)
                    act.sem_inc(set_free[1], 1)
                split_any(split_hi, act, g + PREFETCH, g + PREFETCH)
                s = g - 3 * UP - 3
                if 0 <= s < 12:
                    relu_scores(2 * s)
                    relu_scores(2 * s + 1)
            act.wait_ge(unit_done, u_qk)
            for m in range(2, 4):
                pool_copy(m, main[:, m - 2, :])
            act.wait_ge(pool_u, 4)
            act.sem_inc(set_free[0], 1)

            for part, dst in enumerate((qT, kT)):
                with act.Fori(0, 2) as i:
                    for j in range(2 * UP):
                        split_hi(act, i * (2 * UP) + (u_qk + part * 4 * UP + j + PREFETCH), j + PREFETCH)
                        if j % UP == UP - 1:
                            q = j // UP
                            parity = (p_qk + q) % 2
                            wait_apart(act, unit_done, i * (2 * UP) + (u_qk + part * 4 * UP + j + 1))
                            for m in range(2):
                                act.activation(dst[:, bass.ds(i * 4 + (2 * q + m), 1), :],
                                               main[:, 2 * parity + m:2 * parity + m + 1, :],
                                               ACT.Copy).then_inc(qk_ready, 1)
                            act.wait_ge(qk_ready, i * 4 + (8 * part + 2 * q + 2))
                            act.sem_inc(set_free[parity], 1)

            for n in range(4 * UP):
                if n % UP == 0 and n:
                    v_evict(act, n // UP - 1)
                split_hi(act, u_v + n + PREFETCH, n + PREFETCH)
                if n < 16:
                    src = qT if n < 8 else kT
                    if n == 0:
                        act.wait_ge(pool_diff, NW)
                    if n >= 2:
                        act.wait_ge(sums_done, 1 + n - 1)
                    act.activation(sq[:, n % 2], src[:, n % 8, :], ACT.Square).then_inc(qk_squared, 1)
                if n == 18:
                    act.wait_ge(ms_ready, 2)
                    act.activation(rqk, ms64, ACT.Sqrt).then_inc(root_done, 1)
                if 17 <= n < 17 + NW:
                    gr = n - 17
                    act.wait_ge(pool_mm, gr + 1)
                    act.activation(br_hi[:, gr, :], aux[:, gr % 2, :], ACT.Copy,
                                   scale=cst[:, C_PS + gr:C_PS + gr + 1]).then_inc(a_hi, 1)
            v_evict(act, 3)

            for n in range(6 * UP + 1):
                h, s = n // 6, n % 6
                if n % UP == 0 and n:
                    q = n // UP - 1
                    p = p_att + q
                    if q % 3 == 0:
                        act.wait_ge(unit_done, u_att + n)
                        if q:
                            act.wait_ge(b_lo, 2)
                        for m in range(2):
                            act.activation(cc[:, m], main[:, 2 * (p % 2) + m, :], ACT.Copy).then_inc(cc_ready, 1)
                        act.wait_ge(cc_ready, 2 * (q // 3) + 2)
                        act.sem_inc(set_free[p % 2], 1)
                    elif q % 3 == 2:
                        for m in range(2):
                            act.wait_ge(b_ready, 2 * (q // 3) + m + 1)
                            act.activation(br_hi[:, 4 + 2 * (q // 3) + m, :], cc[:, m], ACT.Copy).then_inc(b_hi, 1)
                if n == 6 * UP:
                    break
                split_hi(act, u_att + n + PREFETCH, n + PREFETCH)
                if s == 1:
                    for n_t, i in enumerate((3, 2, 1, 0)):
                        c = prob_at[i]
                        act.wait_ge(max_ready, 4 * h + n_t + 1)
                        act.activation(prob[:, c:c + P * (i + 1)], prob[:, c:c + P * (i + 1)], ACT.Exp,
                                       bias=nmx[:, i:i + 1], scale=-1.0,
                                       accum_out=rsum[:, i:i + 1]).then_inc(exp_done, 1)
                if s == 5:
                    act.wait_ge(pv_mm, h + 1)
                    act.activation(br_hi[:, 8 + h, :], aux[:, 3, :], ACT.Copy).then_inc(c_hi, 1)
                if s == 4:
                    act.wait_ge(turn_mm, h + 1)
                    if h:
                        act.wait_ge(pv_mm, h)
                    for b in range(2):
                        act.activation(probT[:, b * S:(b + 1) * S], aux[:, b, :], ACT.Copy).then_inc(turned_act, 1)

            def gates(i, last):
                n_gate = 0
                for j in range(G_U):
                    if j in g_ends and g_ends.index(j) % 2 == 0:
                        q = g_ends.index(j)
                        parity = (p_g + q) % 2
                        act.wait_ge(unit_done, i * G_U + (u_g + j))
                        act.wait_ge(gate_used, i * 6 + (2 * n_gate + 1))
                        for m in range(2):
                            act.activation(sg[:, m], main[:, 2 * parity + m, :], ACT.Sigmoid).then_inc(sig_done, 1)
                        act.wait_ge(sig_done, i * 6 + (2 * n_gate + 2))
                        act.sem_inc(set_free[parity], 1)
                        n_gate += 1
                    split_hi(act, i * G_U + (u_g + j + PREFETCH), j + PREFETCH)
                    if last and j >= G_U - 4:
                        for kt in range(4 * (j - G_U + 4), min(4 * (j - G_U + 4) + 4, KT - 2)):
                            act.wait_ge(merged, 2 * kt - 2 * (kt % 2) + 4)
                            act.activation(act_hi[:, kt, :], trunk[:, kt, :], ACT.Copy).then_inc(m_hi, 1)

            with act.Fori(0, G_IT - 1) as i:
                gates(i, False)
            gates(G_IT - 1, True)
            act.wait_ge(merged, G_IT * 4)
            for kt in range(KT - 2, KT):
                act.activation(act_hi[:, kt, :], trunk[:, kt, :], ACT.Copy).then_inc(m_hi, 1)

            for q in range(8):
                act.dma_start(xres[:], xT[q * COLS:(q + 1) * COLS, :].rearrange("(m p) s -> p m s", p=P)
                              ).then_inc(xres_landed, 16)
                for j in range(UP):
                    g = u_o + q * UP + j + PREFETCH
                    split_hi(act, g, g)
                act.wait_ge(x2_ready, 2 * q + 2)
                for m in range(2):
                    t = 2 * q + m
                    act.activation(br_hi[:, t, :], trunk[:, t, :], ACT.Copy,
                                   scale=cst[:, C_G2 + t:C_G2 + t + 1]).then_inc(x2_hi, 1)
                    act.wait_ge(x2_added, t + 1)
                    act.activation(sq[:, 0, :], trunk[:, t, :], ACT.Square).then_inc(x2_squared, 1)

            def up_pass(c, i, q, hook=None):
                for j in range(UP):
                    split_hi(act, c * CH_U + i * (2 * UP) + (u_f + q * UP + j + PREFETCH), j + PREFETCH)
                    if hook:
                        hook(j)
                for m in range(2):
                    t = i * 4 + (2 * q + m)
                    wait_apart(act, f_ready, c * KT + t + 1)
                    act.activation(act_hi[:, bass.ds(t, 1), :], ff[:, m:m + 1, :], ACT.Copy).then_inc(f_hi, 1)

            def norm2_steps(j):
                if j == 3:
                    act.wait_ge(ms_ready, 3)
                    act.activation(r4, ms4, ACT.Sqrt).then_inc(root_done, 1)
                if j == 5:
                    act.wait_ge(bcast_done, 2 + ATTN_HEADS)
                    act.activation(r2B[:, :], aux[:, 0, :], ACT.Copy).then_inc(r2_ready, 1)

            def hidden_chunk(c, first=False, last=False):
                if first:
                    up_pass(0, 0, 0, norm2_steps)
                    up_pass(0, 0, 1)
                with act.Fori(1 if first else 0, 4) as i:
                    up_pass(c, i, 0)
                    up_pass(c, i, 1)
                with act.Fori(0, 7) as i:
                    for j in range(UP):
                        split_hi(act, c * CH_U + i * UP + (u_f + 8 * UP + j + PREFETCH), j + PREFETCH)
                for j in range(UP - PREFETCH if last else UP):
                    split_hi(act, c * CH_U + (u_f + 15 * UP + j + PREFETCH), j + PREFETCH)

            hidden_chunk(0, first=True)
            with act.Fori(1, CH - 1) as c:
                hidden_chunk(c)
            hidden_chunk(CH - 1, last=True)

        @block.vector
        def _(dve):
            chain = Chain(dve, dve_chain)

            def scale_of_tokens(n_sums, n_root, r, ms, tmp, source, width):
                dve.wait_ge(sums_done, n_sums)
                dve.tensor_scalar(ms, source, 1.0 / width, EPS, ALU.mult, ALU.add).then_inc(ms_ready, 1)
                dve.wait_ge(root_done, n_root)
                chain.step(dve.reciprocal(r, r))
                chain.wait()
                chain.step(newton(dve, chain, r, ms, tmp, r))
                chain.wait()

            dve.memset(st[:, 510:512], 0.0).then_inc(st_cleared, 1)

            def xg_tile(kt):
                dve.wait_ge(xg_hi, kt + 1)
                dve.scalar_tensor_tensor(br_lo[:, kt, :], xin[:, kt, :], cst[:, C_G1 + kt:C_G1 + kt + 1],
                                         br_hi[:, kt, :].bitcast(F32), ALU.mult, ALU.subtract).then_inc(xg_lo, 1)

            for kt in range(2 * XG_AHEAD):
                xg_tile(kt)
                if kt % 2:
                    split_any(split_lo, dve, kt // 2, kt // 2)
            for g in range(XG_AHEAD, PREFETCH):
                split_any(split_lo, dve, g, g)

            def scale_h(kt):
                dve.scalar_tensor_tensor(xin[:, kt, :], xin[:, kt, :], cst[:, C_G1 + kt:C_G1 + kt + 1],
                                         rB[:, :], ALU.mult, ALU.mult).then_inc(h_scaled, 1)

            def qi_evict(p):
                for m in range(2):
                    dve.tensor_tensor(qiT[:, 2 * p + m, :], main[:, 2 * p + m, :], rB[:, :],
                                      ALU.mult).then_inc(qi_ready, 1)
                dve.wait_ge(qi_ready, 2 * p + 2)
                dve.sem_inc(set_free[p], 1)

            def add_score(n):
                i, h = 1 + n // 8, n % 8
                dve.wait_ge(relu_done, n + 1)
                if n == 0:
                    dve.wait_ge(ws_ready, 1)
                src = prob[:, (n % 2) * S:(n % 2) * S + P * (i + 1)]
                w = ws[:, i * IDX_HEADS + h:i * IDX_HEADS + h + 1]
                if h == 0:
                    dve.tensor_scalar(score[i - 1][:], src, w, None, ALU.mult).then_inc(score_added, 1)
                else:
                    dve.wait_ge(score_added, n)
                    dve.scalar_tensor_tensor(score[i - 1][:], src, w, score[i - 1][:], ALU.mult,
                                             ALU.add).then_inc(score_added, 1)

            def pool_group(gr):
                m, w = gr % 2, POOL_WINDOWS[gr]
                dve.wait_ge(pool_u, gr + 1)
                cur = U[:, m]
                for s in range(gr + 1):
                    nxt = Sa[:, s % 2]
                    chain.step(dve.tensor_tensor(nxt[:, PADW:], cur[:, PADW:],
                                                 cur[:, PADW - (1 << s):PADW - (1 << s) + S], ALU.add))
                    chain.wait()
                    cur = nxt
                chain.step(dve.tensor_tensor(st[:, 320:336], cur[:, PADW:PADW + 16],
                                             cst[:, C_INV + 16 * gr:C_INV + 16 * gr + 16], ALU.mult))
                chain.step(dve.scalar_tensor_tensor(poolT[:, gr, 16:], cur[:, PADW + 16:], 1.0 / w,
                                                    U[:, m, PADW + 16:], ALU.mult, ALU.subtract))
                chain.wait()
                dve.tensor_tensor(poolT[:, gr, 0:16], st[:, 320:336], U[:, m, PADW:PADW + 16],
                                  ALU.subtract).then_inc(pool_diff, 1)

            for g in range(u_idx, u_qk):
                if g < UP:
                    for kt in range(2 * (g + XG_AHEAD), min(2 * (g + XG_AHEAD) + 2, KT)):
                        xg_tile(kt)
                if g == SUMS_AT:
                    scale_of_tokens(1, 1, r4, ms4, nt4, aux[:, 3, 0:TT], D)
                    diagonals(dve, r4, 0, dg)
                if g == SPREAD_AT:
                    dve.wait_ge(r1_ready, 1)
                    scale_h(0)
                    scale_h(1)
                if g == UP + QI_TILE // 2 + 1:
                    dve.wait_ge(unit_done, g)
                    qi_evict(0)
                if g == 2 * UP:
                    dve.wait_ge(unit_done, g)
                    qi_evict(1)
                n = g - SPREAD_AT
                if 0 <= n < UP:
                    if n + 1 < UP:
                        scale_h(2 * n + 2)
                        scale_h(2 * n + 3)
                    dve.wait_ge(h_hi, 2 * n + 1)
                    dve.tensor_tensor(act_lo[:, 2 * n, :], xin[:, 2 * n, :], act_hi[:, 2 * n, :].bitcast(F32),
                                      ALU.subtract).then_inc(h_lo_even, 1)
                if g == 4 * UP:
                    pool_group(0)
                    pool_group(1)
                split_any(split_lo, dve, g + PREFETCH, g + PREFETCH)
                if g == 3 * UP + 2:
                    dve.wait_ge(wi_turned, 1)
                    dve.tensor_scalar(ws, aux[:, 3, 16:16 + TT * IDX_HEADS], IDX_HEADS ** -0.5, IDX_DIM ** -0.5,
                                      ALU.mult, ALU.mult).then_inc(ws_ready, 1)
                    dve.memset(U[:, :, 0:PADW], 0.0)
                    dve.memset(Sa[:, :, 0:PADW], 0.0).then_inc(pads_ready, 1)
                    dve.wait_ge(pads_ready, 1)
                s = g - 3 * UP - 3
                if 0 <= s < 12:
                    add_score(2 * s)
                    add_score(2 * s + 1)
            dve.wait_ge(score_added, 24)
            for i in (1, 2, 3):
                chain.step(dve.memset(score[i - 1][0:CHUNK, i * P + CHUNK:(i + 1) * P], EMPTY))
            chain.wait()
            for i in (1, 2, 3):
                chain.step(dve.tensor_copy(work[i - 1][:], score[i - 1][:]))
            chain.wait()
            pool_group(2)

            for n in range(8 * UP):
                split_lo(dve, u_qk + n + PREFETCH, n + PREFETCH)
                if n == 0:
                    pool_group(3)
                if n % UP < 6:
                    t = n % UP % 3
                    chain.step(dve.max(top8[t], work[t][:]))
                    chain.wait()
                    chain.step(dve.match_replace(work[t][:], top8[t], work[t][:], EMPTY))
                    chain.wait()

            def mask(t):
                i = t + 1
                n = P * (i + 1)
                dst = maskM[:, prob_at[i]:prob_at[i] + n]
                kth = top8[t][:, 7:8]
                above, equal, rank = dst, work[t][:], prob[:, 0:n]
                chain.step(dve.tensor_scalar(above, score[t][:], kth, None, ALU.is_gt, ALU.add,
                                             accum_out=need[:, t:t + 1]))
                chain.step(dve.tensor_scalar(equal, score[t][:], kth, None, ALU.is_equal))
                chain.wait()
                chain.step(dve.tensor_scalar(need[:, t:t + 1], need[:, t:t + 1], -1.0, float(TOPK), ALU.mult, ALU.add))
                chain.step(dve.tensor_tensor_scan(rank, equal, equal, 0.0, ALU.add, ALU.max))
                chain.wait()
                chain.step(dve.scalar_tensor_tensor(rank, rank, need[:, t:t + 1], equal, ALU.is_le, ALU.mult))
                chain.wait()
                chain.step(dve.tensor_tensor(dst, dst, rank, ALU.add))
                chain.wait()
                return dve.tensor_scalar(dst, dst, -1.0, -MASKED, ALU.add, ALU.mult)

            for n in range(4 * UP):
                split_lo(dve, u_v + n + PREFETCH, n + PREFETCH)
                if n in (0, 2, 4):
                    ins = mask(n // 2)
                    if n == 4:
                        ins.then_inc(topk_done, 1)
                    else:
                        chain.step(ins)
                if n == 6:
                    chain.step(dve.memset(maskM[:, 0:P], 0.0))
                    chain.wait()
                    dve.memset(maskM[0:CHUNK, CHUNK:P], MASKED).then_inc(masks_ready, 1)
                if 17 <= n < 17 + NW:
                    gr = n - 17
                    dve.wait_ge(a_hi, gr + 1)
                    dve.scalar_tensor_tensor(br_lo[:, gr, :], aux[:, gr % 2, :], cst[:, C_PS + gr:C_PS + gr + 1],
                                             br_hi[:, gr, :].bitcast(F32), ALU.mult, ALU.subtract).then_inc(a_lo, 1)
                if n == 17:
                    dve.wait_ge(sums_done, 17)
                    dve.tensor_scalar(ms64, aux[:, 3, 0:64], 1.0 / HD, EPS, ALU.mult, ALU.add).then_inc(ms_ready, 1)
                if n == 22:
                    dve.wait_ge(root_done, 2)
                    chain.step(dve.reciprocal(rqk, rqk))
                    chain.wait()
                    chain.step(newton(dve, chain, rqk, ms64, nt64, rqk))
                    chain.step(dve.tensor_tensor(gqk, cst[:, C_QG:C_QG + 1], cst[:, C_KG:C_KG + 1], ALU.mult))
                    chain.wait()
                    chain.step(dve.tensor_scalar(rqk[:, 0:32], rqk[:, 0:32], -HD ** -0.5, None, ALU.mult))
                    chain.wait()
                if n == 24:
                    diagonals(dve, rqk, 32, dg)

            for n in range(6 * UP + 1):
                h, s = n // 6, n % 6
                q = n // UP - 1
                p = p_att + q
                tile = 2 * (q // 3)
                if n == 3:
                    chain.step(dve.memset(zz[:, :, 0:CONV_K - 1], 0.0))
                if s == 0 and h < ATTN_HEADS:
                    dve.wait_ge(bcast_done, 2 + h)
                    dve.scalar_tensor_tensor(kT[:, h, :], kT[:, h, :], gqk, aux[:, 0, :], ALU.mult,
                                             ALU.mult).then_inc(k_ready, 1)
                if n % UP == 0 and q % 3 == 1:
                    dve.wait_ge(unit_done, u_att + n)
                    dve.wait_ge(cc_ready, tile + 2)
                    for m in range(2):
                        chain.step(dve.tensor_tensor(zz[:, m, CONV_K - 1:], main[:, 2 * (p % 2) + m, :], cc[:, m],
                                                     ALU.mult))
                    chain.wait()
                    dve.sem_inc(set_free[p % 2], 1)
                if n % UP == 0 and n and q % 3 == 2:
                    dve.wait_ge(unit_done, u_att + n)
                    for m in range(2):
                        dve.tensor_tensor(cc[:, m], main[:, 2 * (p % 2) + m, :], cc[:, m], ALU.mult).then_inc(b_ready, 1)
                    dve.wait_ge(b_ready, tile + 2)
                    dve.sem_inc(set_free[p % 2], 1)
                    for m in range(2):
                        dve.wait_ge(b_hi, tile + m + 1)
                        dve.tensor_tensor(br_lo[:, 4 + tile + m, :], cc[:, m], br_hi[:, 4 + tile + m, :].bitcast(F32),
                                          ALU.subtract).then_inc(b_lo, 1)
                if n == 6 * UP:
                    break
                split_lo(dve, u_att + n + PREFETCH, n + PREFETCH)
                if n // UP % 3 == 2 and n % UP in (2, 4):
                    m = n % UP // 2 - 1
                    t = 2 * (n // UP // 3) + m
                    tap = [cst[:, C_CW + 4 * k + t:C_CW + 4 * k + t + 1] for k in range(CONV_K)]
                    chain.step(dve.tensor_scalar(cc[:, m], zz[:, m, 0:S], tap[0], None, ALU.mult))
                    for k in range(1, CONV_K):
                        chain.wait()
                        chain.step(dve.scalar_tensor_tensor(cc[:, m], zz[:, m, k:k + S], tap[k], cc[:, m],
                                                            ALU.mult, ALU.add))
                    chain.wait()
                if s == 5:
                    dve.wait_ge(c_hi, h + 1)
                    dve.tensor_tensor(br_lo[:, 8 + h, :], aux[:, 3, :], br_hi[:, 8 + h, :].bitcast(F32),
                                      ALU.subtract).then_inc(c_lo, 1)
                if s == 1:
                    if h:
                        dve.wait_ge(turn_mm, h)
                    else:
                        dve.wait_ge(masks_ready, 1)
                    for n_t, i in enumerate((3, 2, 1, 0)):
                        bank, c0 = logit_at[i]
                        c = prob_at[i]
                        dve.wait_ge(logits_mm, 4 * h + (1, 3, 4, 4)[n_t])
                        dve.tensor_tensor_reduce(
                            prob[:, c:c + P * (i + 1)], aux[:, bank, c0:c0 + P * (i + 1)], maskM[:, c:c + P * (i + 1)],
                            scale=rqk[:, 4 * h + i:4 * h + i + 1], scalar=-EMPTY, op0=ALU.add, op1=ALU.min,
                            accum_out=nmx[:, i:i + 1]).then_inc(max_ready, 1)
                if s == 2:
                    dve.wait_ge(exp_done, 4 * h + 4)
                    chain.step(dve.reciprocal(rinv, rsum))
                    chain.wait()
                    for i in range(TT):
                        c = prob_at[i]
                        ins = dve.tensor_scalar(prob[:, c:c + P * (i + 1)], prob[:, c:c + P * (i + 1)],
                                                rinv[:, i:i + 1], None, ALU.mult)
                    ins.then_inc(prob_ready, 1)
                    if h + 1 < ATTN_HEADS:
                        dve.wait_ge(bcast_done, 2 + h)
                        diagonals(dve, rqk, 32 + 4 * (h + 1), dg)
                if s == 4:
                    dve.wait_ge(turn_mm, h + 1)
                    if h:
                        dve.wait_ge(pv_mm, h)
                    dve.tensor_copy(probT[:, 2 * S:2 * S + 2 * P], aux[:, 2, 0:2 * P]).then_inc(turned_dve, 1)

            dve.wait_ge(b_lo, 4)
            dve.sem_inc(gate_used, 1)

            def merged_lo(kt):
                dve.wait_ge(m_hi, kt + 1)
                dve.tensor_tensor(act_lo[:, kt, :], trunk[:, kt, :], act_hi[:, kt, :].bitcast(F32),
                                  ALU.subtract).then_inc(m_ready, 1)

            def gates(i, last):
                for j in range(G_U + 1):
                    if j in g_ends and g_ends.index(j) % 2 == 1:
                        q = g_ends.index(j)
                        b, parity = q // 2, (p_g + q) % 2
                        dve.wait_ge(unit_done, i * G_U + (u_g + j))
                        for m in range(2):
                            dve.wait_ge(sig_done, i * 6 + (2 * b + m + 1))
                            t = bass.ds(i * 2 + m, 1)
                            dst = gt[:, m:m + 1, :] if b else trunk[:, t, :]
                            dve.tensor_tensor(dst, main[:, 2 * parity + m:2 * parity + m + 1, :], sg[:, m:m + 1, :],
                                              ALU.mult).then_inc(gate_used, 1)
                        dve.wait_ge(gate_used, i * 6 + (2 * b + 3))
                        dve.sem_inc(set_free[parity], 1)
                        if b == 2:
                            dve.wait_ge(merged, i * 4 + 2)
                        for m in range(2 if b else 0):
                            t = bass.ds(i * 2 + m, 1)
                            dve.tensor_tensor(trunk[:, t, :], trunk[:, t, :], gt[:, m:m + 1, :],
                                              ALU.add).then_inc(merged, 1)
                    if j < G_U:
                        split_lo(dve, i * G_U + (u_g + j + PREFETCH), j + PREFETCH)
                    if last and G_U - 4 <= j < G_U:
                        for kt in range(4 * (j - G_U + 4), min(4 * (j - G_U + 4) + 4, KT - 2)):
                            merged_lo(kt)

            with dve.Fori(0, G_IT - 1) as i:
                gates(i, False)
            gates(G_IT - 1, True)
            merged_lo(KT - 2)
            merged_lo(KT - 1)

            with dve.Fori(0, 4) as i:
                for j in range(2 * UP):
                    split_lo(dve, i * (2 * UP) + (u_o + j + PREFETCH), j + PREFETCH)
                    if j % UP == UP - 1:
                        q = j // UP
                        parity = (p_o + q) % 2
                        dve.wait_ge(unit_done, i * (2 * UP) + (u_o + j + 1))
                        dve.wait_ge(xres_landed, i * 32 + 16 * (q + 1))
                        for m in range(2):
                            t = i * 4 + (2 * q + m)
                            dve.tensor_tensor(trunk[:, bass.ds(t, 1), :], main[:, 2 * parity + m:2 * parity + m + 1, :],
                                              xres[:, m:m + 1, :], ALU.add).then_inc(x2_ready, 1)
                        dve.wait_ge(x2_ready, i * 4 + (2 * q + 2))
                        dve.sem_inc(set_free[parity], 1)
                        for m in range(2):
                            t = i * 4 + (2 * q + m)
                            dve.wait_ge(x2_hi, t + 1)
                            dve.scalar_tensor_tensor(br_lo[:, bass.ds(t, 1), :], trunk[:, bass.ds(t, 1), :],
                                                     cst[:, bass.ds(t + C_G2, 1)],
                                                     br_hi[:, bass.ds(t, 1), :].bitcast(F32),
                                                     ALU.mult, ALU.subtract).then_inc(x2_lo, 1)

            def up_pass(c, i, q, hook=None):
                for j in range(UP):
                    split_lo(dve, c * CH_U + i * (2 * UP) + (u_f + q * UP + j + PREFETCH), j + PREFETCH)
                    if hook:
                        hook(j)
                parity = (p_f + q) % 2
                dve.wait_ge(unit_done, c * CH_U + i * (2 * UP) + (u_f + (q + 1) * UP))
                for m in range(2):
                    dve.tensor_tensor(ft[:, m], main[:, 2 * parity + m, :], r2B[:, :],
                                      ALU.mult).then_inc(f_scaled, 1)
                dve.wait_ge(f_scaled, c * KT + i * 4 + (2 * q + 2))
                dve.sem_inc(set_free[parity], 1)
                for m in range(2):
                    dve.scalar_tensor_tensor(ff[:, m], ft[:, m], 0.0, ft[:, m], ALU.max,
                                             ALU.mult).then_inc(f_ready, 1)
                for m in range(2):
                    t = i * 4 + (2 * q + m)
                    dve.wait_ge(f_hi, c * KT + t + 1)
                    dve.tensor_tensor(act_lo[:, bass.ds(t, 1), :], ff[:, m:m + 1, :],
                                      act_hi[:, bass.ds(t, 1), :].bitcast(F32), ALU.subtract).then_inc(f_lo, 1)

            def norm2_steps(j):
                if j == 3:
                    scale_of_tokens(18, 3, r4, ms4, nt4, aux[:, 3, 0:TT], D)
                    diagonals(dve, r4, 0, ft[:, 1])
                if j == 6:
                    dve.wait_ge(r2_ready, 1)

            def hidden_chunk(c, first=False, last=False):
                if first:
                    up_pass(0, 0, 0, norm2_steps)
                    up_pass(0, 0, 1)
                with dve.Fori(1 if first else 0, 4) as i:
                    up_pass(c, i, 0)
                    up_pass(c, i, 1)

                def y_pass(i, q, n_splits):
                    for j in range(n_splits):
                        split_lo(dve, c * CH_U + i * (2 * UP) + (u_f + (8 + q) * UP + j + PREFETCH), j + PREFETCH)
                    parity = (p_f + q) % 2
                    dve.wait_ge(unit_done, c * CH_U + i * (2 * UP) + (u_f + (9 + q) * UP))
                    for m in range(2):
                        t = bass.ds(i * 4 + (2 * q + m), 1)
                        dve.tensor_tensor(trunk[:, t, :], main[:, 2 * parity + m:2 * parity + m + 1, :], trunk[:, t, :],
                                          ALU.add).then_inc(y_ready, 1)
                    dve.wait_ge(y_ready, c * KT + i * 4 + (2 * q + 2))
                    dve.sem_inc(set_free[parity], 1)

                with dve.Fori(0, 3) as i:
                    y_pass(i, 0, UP)
                    y_pass(i, 1, UP)
                y_pass(3, 0, UP)
                y_pass(3, 1, UP - PREFETCH if last else UP)

            hidden_chunk(0, first=True)
            with dve.Fori(1, CH - 1) as c:
                hidden_chunk(c)
            hidden_chunk(CH - 1, last=True)

        @block.gpsimd
        def _(pool):
            for kt in range(KT):
                pool.wait_ge(x_squared, kt + 1)
                if kt == 0:
                    pool.tensor_copy(dg[:, :], sq[:, 0]).then_inc(x_summed, 1)
                else:
                    pool.wait_ge(x_summed, kt)
                    pool.tensor_tensor(dg[:, :], dg[:, :], sq[:, kt % 2], ALU.add).then_inc(x_summed, 1)

            for kt in range(1, KT, 2):
                pool.wait_ge(h_hi, kt + 1)
                pool.tensor_tensor(act_lo[:, kt, :], xin[:, kt, :], act_hi[:, kt, :].bitcast(F32),
                                   ALU.subtract).then_inc(h_lo_odd, 1)
            pool.wait_ge(k_ready, ATTN_HEADS)
            pool.memset(ssq[:, :], 0.0).then_inc(x2_added, 1)
            with pool.Fori(0, KT) as t:
                pool.wait_ge(x2_squared, t + 1)
                pool.wait_ge(x2_added, t + 1)
                pool.tensor_tensor(ssq[:, :], ssq[:, :], sq[:, 0], ALU.add).then_inc(x2_added, 1)
            for n in range(7):
                pool.wait_ge(y_ready, (CH - 1) * KT + 2 * n + 2)
                pool.dma_start(outT[n * COLS:(n + 1) * COLS, :].rearrange("(m p) s -> p m s", p=P),
                               trunk[:, 2 * n:2 * n + 2, :]).then_inc(out_written, 16)
            pool.wait_ge(out_written, 7 * 16)


def constants(norm1, norm2, pool_scale, conv_w, q_gain, k_gain):
    import numpy as np

    def by_tile(a):
        return np.ascontiguousarray(a).reshape(-1, P).T

    inv = np.array([[1.0 / min(t + 1, w) for w in POOL_WINDOWS for t in range(16)]], np.float32)
    parts = [by_tile(norm1), by_tile(norm2), by_tile(pool_scale), by_tile(conv_w), by_tile(q_gain),
             by_tile(k_gain), np.repeat(inv, P, axis=0), np.eye(P, dtype=np.float32), np.ones((P, P), np.float32)]
    return np.concatenate([np.asarray(a, np.float32) for a in parts], axis=1)


def kernel(**inputs):
    import numpy as np
    import concourse.bacc as bacc
    from concourse.bass_utils import run_bass_kernel_spmd

    a = {k: np.asarray(v) for k, v in inputs.items()}
    x = a["x"]
    arrays = {
        "xT": np.ascontiguousarray(x[0].T),
        "cst": constants(a["norm1"][0], a["norm2"][0], a["pool_scale"][0], a["conv_w"][0], a["q_gain"][0], a["k_gain"][0]),
    }
    for name in ("w_in", "pool_w", "w_pool_out", "w_conv_out", "w_attn_out", "w_o", "w_ff1", "w_ff2"):
        arrays[name] = np.ascontiguousarray(a[name][0])
    nc = bacc.Bacc("TRN2", target_bir_lowering=False, num_devices=1)
    args = [nc.dram_tensor(n, v.shape, mybir.dt.from_np(v.dtype), kind="ExternalInput").ap() for n, v in arrays.items()]
    args.append(nc.dram_tensor("outT", arrays["xT"].shape, F32, kind="ExternalOutput").ap())
    build(nc, *args)
    r = run_bass_kernel_spmd(nc, [arrays], core_ids=[0])
    return np.ascontiguousarray(r.results[0]["outT"].T)[None]
```
